# Optimizing a Trainium2 kernel written in Bass

```python
import jax, jax.numpy as jnp
from jax import lax
import numpy as np

D_MODEL = 2048
BATCH = 1
SEQ = 256
DEPTH = 2

HEAD_DIM = 128
N_HEADS = D_MODEL // HEAD_DIM
N_SB_HEADS = N_HEADS // 2
N_FOX_HEADS = N_HEADS - N_SB_HEADS
Q_BLOCK = 128
POOL_WINDOWS = (2, 4, 8, 16)
N_POOL_GROUPS = len(POOL_WINDOWS)
POOL_GROUP = D_MODEL // N_POOL_GROUPS
D_FF = ((int(8 * D_MODEL / 3) + 255) // 256) * 256
CONV_WIDTH = 3
N_MOD = 6
EPS = 1e-6
N_ATTN_LAYERS = (DEPTH + 1) // 2
N_POOL_LAYERS = DEPTH // 2

kernel_name = "stickbreak_fox_pool_convffn_adaln"

def rms_norm(x, gain):
    xf = x.astype(jnp.float32)
    y = xf * lax.rsqrt(jnp.mean(xf * xf, axis=-1, keepdims=True) + EPS)
    return (y * gain.astype(jnp.float32)).astype(x.dtype)

def modulate(h, shift, scale):
    return h * (1.0 + scale[:, None, :]) + shift[:, None, :]

def attention_mixer(h, w_in, b_forget, w_out):
    B, S, D = h.shape
    proj = h @ w_in
    qkv = proj[..., :3 * D].reshape(B, S, 3, N_HEADS, HEAD_DIM)
    q = qkv[:, :, 0].transpose(0, 2, 1, 3)
    k = qkv[:, :, 1].transpose(0, 2, 1, 3)
    v = qkv[:, :, 2].transpose(0, 2, 1, 3)
    f_logit = proj[..., 3 * D:].astype(jnp.float32) + b_forget.astype(jnp.float32)
    F = jnp.cumsum(jax.nn.log_sigmoid(f_logit), axis=1).transpose(0, 2, 1)
    nb = S // Q_BLOCK
    q_blocks = q.reshape(B, N_HEADS, nb, Q_BLOCK, HEAD_DIM).transpose(2, 0, 1, 3, 4)
    F_blocks = F.reshape(B, N_FOX_HEADS, nb, Q_BLOCK).transpose(2, 0, 1, 3)
    starts = jnp.arange(nb, dtype=jnp.int32) * Q_BLOCK
    s_idx = jnp.arange(S)
    v_sb, v_fx = v[:, :N_SB_HEADS], v[:, N_SB_HEADS:]
    scale = HEAD_DIM ** -0.5

    def block(args):
        qb, Fq, start = args
        t_idx = start + jnp.arange(Q_BLOCK)
        z = jnp.einsum('bhqd,bhkd->bhqk', qb, k).astype(jnp.float32) * scale
        z_sb, z_fx = z[:, :N_SB_HEADS], z[:, N_SB_HEADS:]
        strict = s_idx[None, :] < t_idx[:, None]
        log_rest = jnp.where(strict, jax.nn.log_sigmoid(-z_sb), 0.0)
        log_after = lax.cumsum(log_rest, axis=3, reverse=True) - log_rest
        w_sb = jnp.where(strict, jnp.exp(jax.nn.log_sigmoid(z_sb) + log_after), 0.0)
        o_sb = jnp.einsum('bhqk,bhkd->bhqd', w_sb.astype(v.dtype), v_sb)
        causal = s_idx[None, :] <= t_idx[:, None]
        logits = z_fx + Fq[..., :, None] - F[:, :, None, :]
        p = jax.nn.softmax(jnp.where(causal, logits, -jnp.inf), axis=-1)
        o_fx = jnp.einsum('bhqk,bhkd->bhqd', p.astype(v.dtype), v_fx)
        return jnp.concatenate([o_sb, o_fx], axis=1)

    out = lax.map(block, (q_blocks, F_blocks, starts))
    out = out.transpose(1, 0, 3, 2, 4).reshape(B, S, D)
    return out @ w_out

def pool_mixer(h, w_pool, pool_scale):
    B, S, D = h.shape
    hf = h.astype(jnp.float32).reshape(B, S, N_POOL_GROUPS, POOL_GROUP)
    cs = jnp.cumsum(hf, axis=1)
    pos = jnp.arange(S)
    diffs = []
    for g, w in enumerate(POOL_WINDOWS):
        c_g = cs[:, :, g]
        lagged = jnp.pad(c_g, ((0, 0), (w, 0), (0, 0)))[:, :S]
        count = jnp.minimum(pos + 1, w).astype(jnp.float32)[None, :, None]
        diffs.append((c_g - lagged) / count - hf[:, :, g])
    d = jnp.stack(diffs, axis=2).astype(h.dtype)
    y = jnp.einsum('bsgc,gce->bsge', d, w_pool).reshape(B, S, D)
    return y * pool_scale

def conv_ffn(h, w_up, conv_w, conv_b, w_down):
    S = h.shape[1]
    u = h @ w_up
    up = jnp.pad(u, ((0, 0), (CONV_WIDTH - 1, 0), (0, 0)))
    y = conv_b
    for i in range(CONV_WIDTH):
        y = y + up[:, i:i + S] * conv_w[i]
    a, g = jnp.split(y, 2, axis=-1)
    return (jax.nn.silu(g) * a) @ w_down

def setup_inputs(seed: int = 0) -> dict:
    key = jax.random.key(seed)
    ks = jax.random.split(key, 16)
    n = jax.random.normal
    D, F2 = D_MODEL, 2 * D_FF
    return {
        "x": n(ks[0], (BATCH, SEQ, D), jnp.float32),
        "c": n(ks[1], (BATCH, D), jnp.float32),
        "w_mod": n(ks[2], (DEPTH, D, N_MOD * D), jnp.float32) * (0.5 * D ** -0.5),
        "b_mod": n(ks[3], (DEPTH, N_MOD * D), jnp.float32) * 0.02,
        "norm_gain": 1.0 + 0.1 * n(ks[4], (DEPTH, 2, D), jnp.float32),
        "w_attn_in": n(ks[5], (N_ATTN_LAYERS, D, 3 * D + N_FOX_HEADS), jnp.float32) * D ** -0.5,
        "b_forget": jax.random.uniform(ks[6], (N_ATTN_LAYERS, N_FOX_HEADS), jnp.float32, 1.0, 4.0),
        "w_attn_out": n(ks[7], (N_ATTN_LAYERS, D, D), jnp.float32) * D ** -0.5,
        "w_pool": n(ks[8], (N_POOL_LAYERS, N_POOL_GROUPS, POOL_GROUP, POOL_GROUP), jnp.float32) * POOL_GROUP ** -0.5,
        "pool_scale": 1.0 + 0.1 * n(ks[9], (N_POOL_LAYERS, D), jnp.float32),
        "w_up": n(ks[10], (DEPTH, D, F2), jnp.float32) * D ** -0.5,
        "conv_w": n(ks[11], (DEPTH, CONV_WIDTH, F2), jnp.float32) * CONV_WIDTH ** -0.5,
        "conv_b": n(ks[12], (DEPTH, F2), jnp.float32) * 0.02,
        "w_down": n(ks[13], (DEPTH, D_FF, D), jnp.float32) * D_FF ** -0.5,
        "final_gain": 1.0 + 0.1 * n(ks[14], (D,), jnp.float32),
    }

def reference(x, c, w_mod, b_mod, norm_gain, w_attn_in, b_forget, w_attn_out, w_pool, pool_scale,
              w_up, conv_w, conv_b, w_down, final_gain):
    cond = jax.nn.silu(c)
    for l in range(DEPTH):
        mod = cond @ w_mod[l] + b_mod[l]
        sh1, sc1, g1, sh2, sc2, g2 = jnp.split(mod, N_MOD, axis=-1)
        h = modulate(rms_norm(x, norm_gain[l, 0]), sh1, sc1)
        i = l // 2
        if l % 2 == 0:
            y = attention_mixer(h, w_attn_in[i], b_forget[i], w_attn_out[i])
        else:
            y = pool_mixer(h, w_pool[i], pool_scale[i])
        x = x + g1[:, None, :] * y
        h = modulate(rms_norm(x, norm_gain[l, 1]), sh2, sc2)
        x = x + g2[:, None, :] * conv_ffn(h, w_up[l], conv_w[l], conv_b[l], w_down[l])
    return rms_norm(x, final_gain)


_drawn_inputs = setup_inputs


def setup_inputs(seed=0):
    import zlib

    import numpy as np

    out = dict(_drawn_inputs(seed))
    spreads = {}
    factors = {'conv_b': 7.199}
    for name, (base, spread) in spreads.items():
        noise = np.random.default_rng([zlib.crc32(name.encode()), seed]).standard_normal(out[name].shape)
        drawn = base * np.exp(spread * noise) if base else spread * noise
        out[name] = __import__('jax').numpy.asarray(drawn.astype(out[name].dtype))
    for name, factor in factors.items():
        out[name] = (out[name] * factor).astype(out[name].dtype)
    return out
```

```python
from contextlib import ExitStack

import concourse.bass as bass
from concourse import mybir

ALU = mybir.AluOpType
ACT = mybir.ActivationFunctionType
F32 = mybir.dt.float32
F32R = mybir.dt.float32r
AX_X = mybir.AxisListType.X

P = 128
NEG = -1.0e30
EPS = 1e-6
ds = bass.ds


def decoder_trunk(nc, x, c, w_mod, b_mod, norm_gain, w_attn_in, b_forget, w_attn_out, w_pool,
                  pool_scale, w_up, conv_w, conv_b, w_down, final_gain, out):
    _, SEQ, D = x.shape
    LAYERS = w_mod.shape[0]
    F2 = w_up.shape[2]
    FF = F2 // 2
    NF = b_forget.shape[1]
    HD = 128
    QT = SEQ // P
    KT = D // P
    FT = FF // P
    FT2 = 2 * FT
    assert SEQ == 256 and D == 2048 and LAYERS == 2 and NF == 8 and FT == 44
    SCALE = float(HD) ** -0.5
    NH = D // HD
    NSB = NH - NF

    UNIT_K, UNIT_N = 4, 512
    Q_QKV, Q_OUT, Q_UP, Q_DOWN = 12, 4, 2 * FT // 4, FT // 4
    QUAD_OUT = Q_QKV
    QUAD_FFN = [Q_QKV + Q_OUT, Q_QKV + Q_OUT + Q_UP + Q_DOWN + 1]
    QUAD_POOL = QUAD_FFN[1] - 1
    QUADS = QUAD_FFN[1] + Q_UP + Q_DOWN
    UNITS = 4 * QUADS
    BLOCKS = [(0, 4), (4, 4), (8, 3)]
    G_OUT = Q_QKV
    G_FFN = [G_OUT + 4, G_OUT + 4 + 2 * 11 + 12 + 4]
    G_POOL = G_FFN[1] - 4

    XG = [0, G_OUT, G_FFN[0] + 30, G_POOL, G_FFN[1] + 30]

    CHUNKS = w_mod.shape[2] // 512
    SH1, SC1, G1, SH2, SC2, G2 = [16 * n for n in range(6)]

    with ExitStack() as ctx:
        def sb(name, shape, dt=F32):
            return ctx.enter_context(nc.sbuf_tensor(name, shape, dt))

        def sem(name):
            return ctx.enter_context(nc.semaphore(name))

        xT = sb("xT", [P, KT, SEQ])
        h_hi = sb("h_hi", [P, KT, SEQ], F32R)
        h_lo = sb("h_lo", [P, KT, SEQ], F32R)
        g_hi = sb("g_hi", [P, 16, SEQ], F32R)
        g_lo = sb("g_lo", [P, 16, SEQ], F32R)
        raw = sb("raw", [P, 4, UNIT_K * UNIT_N])
        w_hi = sb("w_hi", [P, 4, 2, UNIT_N], F32R)
        w_lo = sb("w_lo", [P, 4, 2, UNIT_N], F32R)
        mraw = sb("mraw", [P, 4, 2, 512])
        macc = sb("macc", [P, 2, 512])
        prm = sb("prm", [P, 11 * P])
        mods = sb("mods", [P, LAYERS * 96])
        amul = sb("amul", [P, 2 * LAYERS, KT])
        gps = sb("gps", [P, KT])
        cond = sb("cond", [P, KT])
        rstd = sb("rstd", [P, SEQ])
        ident = sb("ident", [P, P])
        ones = sb("ones", [P, P])
        negones = sb("negones", [P, P])
        negtri = sb("negtri", [P, P])
        tri = sb("tri", [P, P])
        keep = sb("keep", [P, 384])
        drop = sb("drop", [P, 384])
        dropf = sb("dropf", [P, 384])
        invw = sb("invw", [P, 16])
        work = sb("work", [P, 6144])
        wf = sb("wf", [P, KT, NF])
        wf_hi = sb("wf_hi", [P, KT, NF], F32R)
        wf_lo = sb("wf_lo", [P, KT, NF], F32R)
        bfb = sb("bfb", [P, NF])
        fg = sb("fg", [P, 4, QT, NF])
        nls = sb("nls", [P, QT, NF])
        Fq = sb("Fq", [P, NF, QT])
        fst = sb("fst", [P, 5, NF, QT])

        ps = ctx.enter_context(nc.psum_tensor("ps", [P, 8, 512], F32))

        x_tok = work[:, 0:4096].rearrange("p (a n) -> p a n", a=QT)
        prow = work[:, 4096:4096 + 11 * P]
        kT = work[:, 0:1024].rearrange("p (h t) -> p h t", h=4)
        qT = work[:, 1024:2048].rearrange("p (h t) -> p h t", h=4)
        vv = work[:, 2048:3072].rearrange("p (a n) -> p a n", a=QT)
        att = work[:, 3072:3072 + 8 * 384].rearrange("p (b n) -> p b n", b=8)
        ya = work[:, 0:1024].rearrange("p (t n) -> p t n", t=4)
        yg = work[:, 1024:2048].rearrange("p (t n) -> p t n", t=4)
        hp = work[:, 0:1024].rearrange("p (t n) -> p t n", t=4)
        sA = work[:, 1024:2048].rearrange("p (t n) -> p t n", t=4)
        sB = work[:, 2048:3072].rearrange("p (t n) -> p t n", t=4)
        sq = work[:, 4096:6144].rearrange("p (b t n) -> p b t n", b=2, t=4)
        tmpn = work[:, 3072:4096].rearrange("p (t n) -> p t n", t=4)
        o_tok = raw[:, 0:2, :]
        CWcol = lambda l, i: (3 + 3 * l + i) * P
        CBcol = lambda l: (9 + l) * P
        GAIN, PSC, FGAIN = 16, 80, 96

        def bank_tile(g2, t):
            return ps[:, 2 * g2 + t // 2, (t % 2) * 256:(t % 2) * 256 + 256]

        s_prm = [sem(f"prm_landed{n}") for n in range(3)]
        s_x = sem("x_landed")
        s_wf = sem("wf_landed")
        raw_landed = [sem(f"raw_landed{n}") for n in range(4)]
        mod_landed = [sem(f"mod_landed{n}") for n in range(4)]
        consts = sem("consts")
        prm_t = sem("prm_transposed")
        prm_ready = sem("prm_ready")
        x_t = sem("x_transposed")
        x_copied = sem("x_copied")
        cond_s = sem("cond_silu")
        hi_ready = sem("hi_ready")
        lo_ready = sem("lo_ready")
        sub_used = sem("sub_used")
        bank0_free = sem("bank0_free")
        bank1_free = sem("bank1_free")
        mod_acc = sem("mod_acc")
        mod_red = sem("mod_reduced")
        mod_ready = sem("mod_ready")
        sq_ready = sem("sq_ready")
        sum_done = sem("sum_done")
        ms_ready = sem("ms_ready")
        rt_ready = sem("rt_ready")
        t_ready = sem("t_ready")
        hhi_ready = sem("hhi_ready")
        hlo_ready = sem("hlo_ready")
        wf_split = sem("wf_split")
        wf_hi_s = sem("wf_hi")
        f_done = sem("f_done")
        f_act = sem("f_act")
        f_dve = sem("f_dve")
        z_done = sem("z_done")
        sb_act = sem("sb_act")
        l_ready = sem("l_ready")
        sp_ready = sem("sp_ready")
        cum_done = sem("cum_done")
        w_ready = sem("w_ready")
        bias_ready = sem("bias_ready")
        p_exp = sem("p_exp")
        p_ready = sem("p_ready")
        att_free = sem("att_free")
        o_done = sem("o_done")
        o_hi = sem("o_hi")
        o_lo = sem("o_lo")
        conv_act = sem("conv_act")
        conv_tap = sem("conv_tap")
        silu_done = sem("silu_done")
        gg_ready = sem("gg_ready")
        ghi_ready = sem("ghi_ready")
        glo_ready = sem("glo_ready")
        hp_ready = sem("hp_ready")
        pool_step = sem("pool_step")
        y_t = sem("y_transposed")
        y_cp = sem("y_copied")
        dve_step = sem("dve_step")
        s_out = sem("out_stored")

        SCHED = {}
        for hg in range(4):
            base = 12 * (hg + 1)
            if hg < 2:
                a, b, o = [0, 1, 2, 4], [2, 3, 4, 6], [4, 5, 6, 8]
            elif hg == 2:
                a, b, o = [0, 1, 2, 3], [2, 3, 4, 5], [4, 5, 6, 7]
            else:
                a, b, o = [0, 0, 1, 1], [2, 2, 3, 3], [4, 4, 5, 5]
            for n in range(4):
                for kind, at in (("z", a[n]), ("c", b[n]), ("o", o[n])):
                    SCHED.setdefault(base + at, []).append((kind, 4 * hg + n))
        ORDER = {"z": 0, "c": 1, "o": 2}
        for v in SCHED.values():
            v.sort(key=lambda s: (ORDER[s[0]], s[1]))
        ALLOC = {}
        for pos in sorted(SCHED):
            for kind, n in SCHED[pos]:
                if kind == "z" or (kind == "c" and n >= NSB):
                    ALLOC[(kind, n)] = len(ALLOC)

        def att_bank(key):
            return ps[:, 4 + ALLOC[key] % 3, 0:384]

        def out_bank(n):
            return ps[:, 4 if n in (13, 15) else 7, 0:256]
        assert ALLOC[("c", 13)] % 3 == 0

        def weights_buf(n):
            return att[:, 4 + (n % 2 if n < NSB else n % 4), :]

        def qkv_unit(pos):
            hg, j = divmod(pos, 12)
            return hg, "kqv"[j // 4], j % 4
        OUT_UNITS = [(0, 0), (0, 1), (0, 2), (1, 0), (1, 1), (1, 2), (0, 3), (1, 3)] + \
                    [(cg, ks) for cg in (2, 3) for ks in range(4)]

        def mod_at(pos):
            return 8 + pos // 4, [2 * (pos % 4), 2 * (pos % 4) + 1]

        MOD_SUM = {7: 8, 19: 11, 31: 14, 44: 17, 54: 20}
        MOD_SUM.update({4 * n + 5: 8 + n for n in range(15) if n % 3})
        assert sorted(MOD_SUM[p] for p in MOD_SUM) == [MOD_SUM[p] for p in sorted(MOD_SUM)]
        mod_sum_at = MOD_SUM.get

        def o_before(pos):
            return sum(1 for q in SCHED if q < pos for s in SCHED[q] if s[0] == "o")

        MODS = {pos: 8 + sum(1 for p in range(pos) if mod_sum_at(p) is not None) for pos in range(64)}

        block = ctx.enter_context(nc.Block())

        @block.sync
        def _(sp):
            def rows(v):
                return v.rearrange("(r p) -> r p", p=P)
            for n, (v, r0) in enumerate(((c[0], 0), (pool_scale[0], PSC), (final_gain, FGAIN))):
                sp.dma_start(prow[r0:r0 + KT, 0:P], rows(v)).then_inc(s_prm[0], 16)
            sp.dma_start(prow[GAIN:GAIN + 64, 0:P],
                         norm_gain.rearrange("l a (r p) -> (l a r) p", p=P)).then_inc(s_prm[0], 16)
            for l in range(LAYERS):
                sp.dma_start(prow[0:96, (1 + l) * P:(2 + l) * P], rows(b_mod[l])).then_inc(s_prm[1], 16)
                for i in range(3):
                    sp.dma_start(prow[0:FT2, CWcol(l, i):CWcol(l, i) + P], rows(conv_w[l, i])).then_inc(s_prm[1], 16)
                sp.dma_start(prow[0:FT2, CBcol(l):CBcol(l) + P], rows(conv_b[l])).then_inc(s_prm[1], 16)
            sp.dma_start(x_tok, x[0].rearrange("(a p) n -> p a n", p=P)).then_inc(s_x, 16)
            with nc.allow_non_contiguous_dma("the eight forget columns, the bias on every partition"):
                sp.dma_start(wf[:, :, :], w_attn_in[0, :, 3 * D:3 * D + NF]
                             .rearrange("(k p) n -> p k n", p=P)).then_inc(s_wf, 16)
                sp.dma_start(bfb[:, :], b_forget[0:1, :].partition_broadcast(P)
                             if hasattr(b_forget, "partition_broadcast") else b_forget[0:1, :].to_broadcast([P, NF])).then_inc(s_wf, 16)

            def load(q, j, src):
                if not (isinstance(q, int) and q == 0):
                    sp.wait_ge(lo_ready, 8 * q + 2 * j - 6)
                sp.dma_start(raw[:, j % 4, :].rearrange("p (k n) -> p k n", k=UNIT_K),
                             src.rearrange("(k p) n -> p k n", p=P)).then_inc(raw_landed[j % 4], 16)

            for pos in range(48):
                hg, kind, ks = qkv_unit(pos)
                col = {"q": 0, "k": D, "v": 2 * D}[kind] + 512 * hg
                load(pos // 4, pos % 4, w_attn_in[0, 512 * ks:512 * ks + 512, col:col + 512])
            for n, (cg, ks) in enumerate(OUT_UNITS):
                load(QUAD_OUT + n // 4, n % 4,
                     w_attn_out[0, 512 * ks:512 * ks + 512, 512 * cg:512 * cg + 512])
            for l in range(LAYERS):
                if l == 1:
                    for g in range(4):
                        load(QUAD_POOL, g, w_pool[0, g])
                q = QUAD_FFN[l]
                for g0, n in BLOCKS:
                    with sp.Fori(0, n) as i:
                        for half in range(2):
                            for ks in range(4):
                                load(q + 2 * i + half, ks,
                                     w_up[l, 512 * ks:512 * ks + 512, ds(half * FF + 512 * g0 + 512 * i, 512)])
                    q += 2 * n
                    if n == 4:
                        with sp.Fori(0, 4) as i:
                            for ks in range(4):
                                load(q + i, ks, w_down[l, 512 * (g0 + ks):512 * (g0 + ks) + 512, ds(512 * i, 512)])
                        q += 4
                    else:
                        for cg in range(4):
                            for ks in range(3):
                                u = 3 * cg + ks
                                load(q + u // 4, u % 4,
                                     w_down[l, 512 * (g0 + ks):512 * (g0 + ks) + 512, 512 * cg:512 * cg + 512])
                        q += 3
            for a in range(QT):
                sp.wait_ge(y_cp, 4 * (a + 1))
                sp.dma_start(out[0, a * P:(a + 1) * P, :], o_tok[:, a, :]).then_inc(s_out, 16)
            sp.wait_ge(s_out, 16 * QT)

        @block.gpsimd
        def _(pool):
            NCONST = 0
            for t, v in ((ident, 0.0), (ones, 1.0), (negones, -1.0), (negtri, -1.0), (tri, 1.0),
                         (keep, 1.0), (drop, 0.0), (dropf, 0.0)):
                pool.memset(t[:, :], v).then_inc(consts, 1)
                NCONST += 1
            for t in range(16):
                pool.memset(invw[:, t:t + 1], 1.0 / (t + 1)).then_inc(consts, 1)
                NCONST += 1
            pool.wait_ge(consts, NCONST)

            def select(t, cmp, fill, base, cm, step):
                pool.affine_select(out=t, in_=t, compare_op=cmp, fill=fill, base=base,
                                   pattern=[[step, P]], channel_multiplier=cm).then_inc(consts, 1)
            select(ident[:, :], ALU.not_equal, 1.0, 0, 1, -1)
            select(negtri[:, :], ALU.is_ge, 0.0, 0, 1, -1)
            select(tri[:, :], ALU.is_ge, 0.0, 0, -1, 1)
            for c0 in (0, 256):
                select(keep[:, c0:c0 + P], ALU.is_gt, 0.0, 0, -1, 1)
                select(drop[:, c0:c0 + P], ALU.is_gt, NEG, 0, -1, 1)
                select(dropf[:, c0:c0 + P], ALU.is_ge, NEG, 0, 1, -1)

            def piece(l, c_all, c_l, j):
                if not (isinstance(c_all, int) and 8 * c_all + j < 4):
                    pool.wait_ge(mod_acc, 16 * c_all + 2 * j - 6)
                pool.dma_start(mraw[:, j % 4, :, :],
                               w_mod[l, 256 * j:256 * j + 256, ds(512 * c_l, 512)]
                               .rearrange("(k p) n -> p k n", p=P)).then_inc(mod_landed[j % 4], 16)
            for j in range(8):
                piece(0, 0, 0, j)
            with pool.Fori(1, CHUNKS) as i:
                for j in range(8):
                    piece(0, i, i, j)
            with pool.Fori(0, CHUNKS) as i:
                for j in range(8):
                    piece(1, i + CHUNKS, i, j)

        ALL_CONSTS = 8 + 16 + 3 + 6

        @block.tensor
        def _(pe):
            mm = nc.tensor.matmul

            def sub(q, j, h, k, last_half, first, act_hi, act_lo, g2):
                pe.wait_ge(lo_ready, 8 * q + 2 * j + h + 1)
                s = (2 * j + h) % 4
                for kk in range(2):
                    for t in range(4):
                        o = bank_tile(g2, t)
                        wh, wl = (w[:, s, kk, t * P:(t + 1) * P] for w in (w_hi, w_lo))
                        ah, al = act_hi[:, k + kk, :], act_lo[:, k + kk, :]
                        st = first and kk == 0 and t % 2 == 0
                        mm(o, wh, ah, start=st, stop=False, skip_group_check=True)
                        mm(o, wh, al, start=False, stop=False, skip_group_check=True)
                        i = mm(o, wl, ah, start=False, stop=last_half and kk == 1, skip_group_check=True)
                i.then_inc(sub_used, 1)

            def unit(q, j, k0, first, last, act_hi, act_lo, g2, h_need=None):
                for h in range(2):
                    if h_need is not None:
                        pe.wait_ge(hlo_ready, h_need + k0 + 2 * h + 2)
                    sub(q, j, h, k0 + 2 * h, last and h == 1, first and h == 0, act_hi, act_lo, g2)

            def unit_tok(q, j, k0, first, last, g2):
                for h in range(2):
                    pe.wait_ge(lo_ready, 8 * q + 2 * j + h + 1)
                    s = (2 * j + h) % 4
                    for kk in range(2):
                        k = k0 + 2 * h + kk
                        for a in range(QT):
                            o = ps[:, 2 * g2 + a, :]
                            ah, al = (w[:, k, a * P:(a + 1) * P] for w in (h_hi, h_lo))
                            st = first and h == 0 and kk == 0
                            sp_ = last and h == 1 and kk == 1
                            mm(o, ah, w_hi[:, s, kk, :], start=st, stop=False)
                            mm(o, ah, w_lo[:, s, kk, :], start=False, stop=False)
                            i = mm(o, al, w_hi[:, s, kk, :], start=False, stop=sp_)
                    i.then_inc(sub_used, 1)

            def group_slot_free(g):
                pe.wait_ge(bank0_free, g - 1)
                pe.wait_ge(bank1_free, g - 1)

            def mod_sum(c_all, a, o_written):
                pe.wait_ge(mod_acc, 16 * c_all + 16)
                if not (isinstance(c_all, int) and c_all == 0):
                    pe.wait_ge(mod_ready, c_all)
                if o_written:
                    pe.wait_ge(o_lo, o_written)
                for t in range(4):
                    i = mm(ps[:, 7, 256 + t:257 + t], macc[:, a, t * P:(t + 1) * P], ones[:, 0:1],
                           start=True, stop=True)
                i.then_inc(mod_red, 1)

            def sum_squares(n, q):
                pe.wait_ge(sq_ready, 4 * n + q + 1)
                for t in range(4):
                    i = mm(ps[:, 6, 0:SEQ], ones[:, :], sq[:, q % 2, t, :],
                           start=(q == 0 and t == 0), stop=(q == 3 and t == 3))
                i.then_inc(sum_done, 1)

            pe.wait_ge(consts, ALL_CONSTS)
            pe.wait_ge(s_prm[0], 64)
            pe.wait_ge(s_prm[1], 16 * 10)
            ROWS = [112, 96, 96] + [FT2] * 8
            for b in range(11):
                i = nc.tensor.transpose(ps[:, 4 + b // 4, (b % 4) * P:(b % 4) * P + ROWS[b]],
                                        prow[0:ROWS[b], b * P:(b + 1) * P], ident[0:ROWS[b], 0:ROWS[b]])
                if b in (3, 7, 10):
                    i.then_inc(prm_t, 1)
            pe.wait_ge(s_x, 16)
            for b in range(8):
                if b >= 4:
                    pe.wait_ge(x_copied, b - 3)
                for t in range(2):
                    for a in range(QT):
                        k = 2 * b + t
                        i = nc.tensor.transpose(ps[:, b % 4, (2 * t + a) * P:(2 * t + a + 1) * P],
                                                x_tok[:, a, k * P:(k + 1) * P], ident[:, :])
                i.then_inc(x_t, 1)
            pe.wait_ge(prm_ready, 3)
            for q in range(4):
                sum_squares(0, q)
            with pe.Fori(0, 4) as i:
                for a in (1, 0):
                    cc = 2 * i + (1 - a)
                    pe.wait_ge(mod_acc, 16 * cc + 16)
                    pe.wait_ge(mod_ready, cc)
                    for t in range(4):
                        m = mm(ps[:, 7, 256 + t:257 + t], macc[:, a, t * P:(t + 1) * P], ones[:, 0:1],
                               start=True, stop=True)
                    m.then_inc(mod_red, 1)

            def scores(n):
                pe.wait_ge(bank0_free, 3 * (n // 4 + 1))
                pe.wait_ge(bank1_free, 3 * (n // 4 + 1))
                if ALLOC[("z", n)] >= 3:
                    pe.wait_ge(att_free, ALLOC[("z", n)] - 2)
                z = att_bank(("z", n))
                k, q = kT[:, n % 4, :], qT[:, n % 4, :]
                if n < NSB:
                    mm(z[:, 0:256], k[:, 0:P], q, start=True, stop=False, skip_group_check=True)
                    i = mm(z[:, 256:384], k[:, P:2 * P], q[:, P:2 * P], start=False, stop=True, skip_group_check=True)
                else:
                    f = n - NSB
                    mm(z[:, 0:P], q[:, 0:P], k[:, 0:P], start=True, stop=False, skip_group_check=True)
                    mm(z[:, P:384], q[:, P:2 * P], k, start=False, stop=False, skip_group_check=True)
                    b0, b1 = (nls[:, a, f:f + 1].to_broadcast([P, P]) for a in range(QT))
                    mm(z[:, 0:P], b0, tri[:, :], start=False, stop=False, skip_group_check=True)
                    mm(z[:, P:2 * P], b0, tri[:, :], start=False, stop=False, skip_group_check=True)
                    mm(z[:, 2 * P:384], b0, ones[:, :], start=False, stop=False, skip_group_check=True)
                    i = mm(z[:, 2 * P:384], b1, tri[:, :], start=False, stop=True, skip_group_check=True)
                i.then_inc(z_done, 1)

            def suffix_sums(n):
                z = att_bank(("z", n))
                spn = att[:, 2 + n % 2, :]
                pe.wait_ge(sp_ready, n + 1)
                mm(z[:, 0:256], negtri[:, :], spn[:, 0:256], start=False, stop=False, skip_group_check=True)
                mm(z[:, P:256], negones[:, :], spn[:, 256:384], start=False, stop=False, skip_group_check=True)
                mm(z[:, 256:384], negtri[:, :], spn[:, 256:384], start=False, stop=True,
                   skip_group_check=True).then_inc(cum_done, 1)

            def flip_probs(n):
                f = n - NSB
                pe.wait_ge(p_ready, f + 1)
                pe.wait_ge(att_free, ALLOC[("c", n)] - 2)
                o = att_bank(("c", n))
                for b in range(3):
                    i = nc.tensor.transpose(o[:, b * P:(b + 1) * P], att[:, f % 4, b * P:(b + 1) * P], ident[:, :])
                i.then_inc(cum_done, 1)

            def head_out(n, mods_written):
                if n < NSB:
                    pe.wait_ge(w_ready, n + 1)
                else:
                    pe.wait_ge(att_free, ALLOC[("c", n)] + 1)
                if n >= 13:
                    pe.wait_ge(att_free, ALLOC[("c", 13)] + 1)
                    pe.wait_ge(o_lo, n - 1)
                elif n:
                    pe.wait_ge(o_lo, n)
                pe.wait_ge(mod_ready, mods_written)
                w = weights_buf(n)
                v0, v1 = (vv[:, a, (n % 4) * HD:(n % 4 + 1) * HD] for a in range(QT))
                mm(out_bank(n), v0, w[:, 0:256], start=True, stop=False)
                mm(out_bank(n)[:, P:256], v1, w[:, 256:384], start=False, stop=True).then_inc(o_done, 1)

            def forget_logits():
                pe.wait_ge(wf_split, 1)
                pe.wait_ge(hlo_ready, KT)
                for a in range(QT):
                    for k in range(KT):
                        ah, al = (w[:, k, a * P:(a + 1) * P] for w in (h_hi, h_lo))
                        o = ps[:, 6, a * NF:(a + 1) * NF]
                        mm(o, ah, wf_hi[:, k, :], start=(k == 0), stop=False)
                        mm(o, ah, wf_lo[:, k, :], start=False, stop=False)
                        i = mm(o, al, wf_hi[:, k, :], start=False, stop=(k == KT - 1))
                i.then_inc(f_done, 1)

            def forget_sums():
                pe.wait_ge(f_dve, 2)
                mm(ps[:, 6, 0:NF], tri[:, :], nls[:, 0, :], start=True, stop=True)
                mm(ps[:, 6, NF:2 * NF], ones[:, :], nls[:, 0, :], start=True, stop=False)
                mm(ps[:, 6, NF:2 * NF], tri[:, :], nls[:, 1, :], start=False, stop=True).then_inc(f_done, 1)

            def attention_steps(pos):
                if pos == 4:
                    forget_logits()
                if pos == 7:
                    forget_sums()
                if pos == 12:
                    pe.wait_ge(f_dve, 3)
                for kind, n in SCHED.get(pos, []):
                    if kind == "z":
                        scores(n)
                    elif kind == "c":
                        (suffix_sums if n < NSB else flip_probs)(n)
                    else:
                        head_out(n, MODS[pos])
                if mod_sum_at(pos) is not None:
                    ch = mod_sum_at(pos)
                    mod_sum(ch, (ch + 1) % 2, o_before(pos))

            for pos in range(48):
                attention_steps(pos)
                hg, kind, ks = qkv_unit(pos)
                g = pos // 4
                if ks == 0 and g >= 2:
                    group_slot_free(g)
                if kind == "v":
                    unit_tok(pos // 4, pos % 4, 4 * ks, ks == 0, ks == 3, g % 2)
                else:
                    unit(pos // 4, pos % 4, 4 * ks, ks == 0, ks == 3, h_hi, h_lo, g % 2,
                         h_need=0 if pos < 4 else None)
            for n, (cg, ks) in enumerate(OUT_UNITS):
                pos = 48 + n
                attention_steps(pos)
                if n == 9:
                    sum_squares(1, 0)
                if n == 10:
                    sum_squares(1, 1)
                if n == 14:
                    sum_squares(1, 2)
                if ks == 0:
                    group_slot_free(G_OUT + cg)
                pe.wait_ge(o_lo, 4 * (ks + 1))
                unit(QUAD_OUT + n // 4, n % 4, 4 * ks, ks == 0, ks == 3, g_hi, g_lo, cg % 2)
            mod_sum(8 + 15, 0, NH)
            sum_squares(1, 3)

            def mlp(l):
                q, g, nrm = QUAD_FFN[l], G_FFN[l], 2 * l + 1
                ch = 24 if l == 0 else 44
                gi = 11 * l
                for g0, n in BLOCKS:
                    last_block = n == 3
                    with_mod = l == 0 or g0 == 0
                    with pe.Fori(0, n) as i:
                        for half in range(2):
                            group_slot_free(g + 2 * i + half)
                            for ks in range(4):
                                if with_mod and half == 1 and ks == 2:
                                    mod_sum(i + ch, 0, NH)
                                unit(q + 2 * i + half, ks, 4 * ks, ks == 0, ks == 3, h_hi, h_lo, half,
                                     h_need=KT * nrm)
                    q += 2 * n
                    g += 2 * n
                    if with_mod:
                        ch += n
                    if not last_block:
                        with pe.Fori(0, 2) as i:
                            for half in range(2):
                                group_slot_free(g + 2 * i + half)
                                for ks in range(4):
                                    if l == 0 and (half, ks) in ((1, 0), (1, 3)):
                                        a = 1 if ks == 0 else 0
                                        mod_sum(2 * i + (ch + (1 - a)), a, NH)
                                    pe.wait_ge(glo_ready, 2 * (gi + g0 + ks + 1))
                                    unit(q + 2 * i + half, ks, 4 * ks, ks == 0, ks == 3, g_hi, g_lo, half)
                        q += 4
                        g += 4
                        if l == 0:
                            ch += 4
                    else:
                        for cg in range(4):
                            group_slot_free(g + cg)
                            for ks in range(3):
                                u = 3 * cg + ks
                                if u in (5, 8, 11):
                                    sum_squares(2 * l + 2, (u - 5) // 3)
                                if l == 0 and u == 5:
                                    mod_sum(ch, 0, NH)
                                pe.wait_ge(glo_ready, 2 * (gi + g0 + ks + 1))
                                unit(q + u // 4, u % 4, 4 * ks, ks == 0, ks == 2, g_hi, g_lo, cg % 2)
                sum_squares(2 * l + 2, 3)

            mlp(0)
            for gr in range(4):
                group_slot_free(G_POOL + gr)
                for h in range(2):
                    pe.wait_ge(hlo_ready, 2 * KT + 4 * gr + 4)
                    sub(QUAD_POOL, gr, h, 4 * gr + 2 * h, h == 1, h == 0, h_hi, h_lo, gr % 2)
            for q in range(4):
                sum_squares(3, q)
            mlp(1)
            for b in range(8):
                a, k0 = b // 4, 4 * (b % 4)
                pe.wait_ge(t_ready, 4 * KT + k0 + 4)
                if b >= 4:
                    pe.wait_ge(y_cp, b - 3)
                else:
                    pe.wait_ge(bank1_free, G_FFN[1] + 34)
                for t in range(4):
                    i = nc.tensor.transpose(ps[:, b % 4, t * P:(t + 1) * P],
                                            xT[:, k0 + t, a * P:(a + 1) * P], ident[:, :])
                i.then_inc(y_t, 1)

        @block.scalar
        def _(act):
            def A(o, i, f, **kw):
                return nc.scalar.activation(o, i, f, **kw)

            def split(q, j):
                act.wait_ge(raw_landed[j % 4], 16 * (q + j // 4 + 1))
                for h in range(2):
                    if not (isinstance(q, int) and 8 * q + 2 * j + h < 4):
                        act.wait_ge(sub_used, 8 * q + 2 * j + h - 3)
                    A(w_hi[:, (2 * j + h) % 4, :, :],
                      raw[:, j % 4, h * 1024:(h + 1) * 1024].rearrange("p (k n) -> p k n", k=2),
                      ACT.Copy).then_inc(hi_ready, 1)

            def squares(n, q):
                if n == 0:
                    act.wait_ge(x_copied, 2 * (q + 1))
                else:
                    act.wait_ge(bank1_free, XG[n] + q + 1)
                if 4 * n + q >= 2:
                    act.wait_ge(sum_done, 4 * n + q - 1)
                A(sq[:, q % 2, :, :], xT[:, 4 * q:4 * q + 4, :], ACT.Square).then_inc(sq_ready, 1)

            def root(n):
                act.wait_ge(ms_ready, n + 1)
                A(rstd[:, :], rstd[:, :], ACT.Sqrt).then_inc(rt_ready, 1)

            def modulate(n):
                l, m = n // 2, n % 2
                sh = 96 * l + (SH2 if m else SH1)
                act.wait_ge(mod_ready, 24 * l + (16 if m else 4))
                for t in range(KT):
                    act.wait_ge(t_ready, n * KT + t + 1)
                    A(h_hi[:, t, :], tmpn[:, t % 4, :], ACT.Identity,
                      bias=mods[:, sh + t:sh + t + 1]).then_inc(hhi_ready, 1)

            act.wait_ge(prm_ready, 1)
            A(cond[:, :], prm[:, 0:KT], ACT.Silu).then_inc(cond_s, 1)
            for q in range(4):
                squares(0, q)
            root(0)
            act.wait_ge(s_wf, 32)
            A(wf_hi[:, :, :], wf[:, :, :], ACT.Copy).then_inc(wf_hi_s, 1)
            split(0, 0)
            split(0, 1)
            modulate(0)

            def softplus_tail(n):
                z, L = att_bank(("z", n)), att[:, n % 2, :]
                act.wait_ge(z_done, n + 1)
                if n >= 2:
                    act.wait_ge(sp_ready, n - 1)
                A(L, z, ACT.Abs).then_inc(sb_act, 1)
                act.wait_ge(sb_act, 2 * n + 1)
                A(L, L, ACT.Exp, scale=-1.0).then_inc(sb_act, 1)
                act.wait_ge(sb_act, 2 * n + 2)
                A(L, L, ACT.Ln, bias=1.0).then_inc(l_ready, 1)

            def softmax_exp(n):
                f = n - NSB
                act.wait_ge(bias_ready, f + 1)
                for a, (lo, hi) in enumerate(((0, P), (P, 384))):
                    A(att[:, f % 4, lo:hi], att[:, f % 4, lo:hi], ACT.Exp, bias=fst[:, 2, f, a:a + 1],
                      accum_out=fst[:, 3, f, a:a + 1]).then_inc(p_exp, 1)

            def stick_weights(n):
                act.wait_ge(att_free, ALLOC[("z", n)] + 1)
                A(weights_buf(n), weights_buf(n), ACT.Exp).then_inc(w_ready, 1)

            def head_hi(n):
                act.wait_ge(o_done, n + 1)
                A(g_hi[:, n, :], out_bank(n), ACT.Copy).then_inc(o_hi, 1)

            def attention_steps(pos):
                if pos == 5:
                    act.wait_ge(f_dve, 1)
                    A(fg[:, 1], fg[:, 0], ACT.Abs).then_inc(f_act, 1)
                    act.wait_ge(f_act, 1)
                    A(fg[:, 2], fg[:, 1], ACT.Exp, scale=-1.0).then_inc(f_act, 1)
                    act.wait_ge(f_act, 2)
                    A(fg[:, 3], fg[:, 2], ACT.Ln, bias=1.0).then_inc(f_act, 1)
                for kind, n in SCHED.get(pos, []):
                    if kind == "z":
                        (softplus_tail if n < NSB else softmax_exp)(n)
                    elif kind == "c" and n < NSB:
                        stick_weights(n)
                    elif kind == "o":
                        head_hi(n)

            for pos in range(64):
                split((pos + 2) // 4, (pos + 2) % 4)
                attention_steps(pos)
                if pos < 48 and pos % 4 == 3:
                    g = pos // 4
                    hg, kind, _ks = qkv_unit(pos)
                    dst = {"k": kT, "q": qT, "v": vv}[kind].rearrange("p a b -> p (a b)")[:, 0:512]
                    act.wait_ge(sub_used, 8 * (g + 1))
                    if hg:
                        if kind == "v":
                            act.wait_ge(o_done, 4 * hg)
                        else:
                            act.wait_ge(z_done, 4 * hg)
                    A(dst, ps[:, 2 * (g % 2), :], ACT.Copy,
                      scale=SCALE if kind == "q" else 1.0).then_inc(bank0_free, 1)
                n = pos - 48
                if n in (6, 7, 11, 15):
                    squares(1, {6: 0, 7: 1, 11: 2, 15: 3}[n])

            def conv_last_tap(l, used, dst, first_tile, slot, need):
                act.wait_ge(sub_used, used)
                act.wait_ge(gg_ready, need)
                for t in range(4):
                    A(dst[:, t, :], bank_tile(slot, t), ACT.Identity,
                      scale=prm[:, ds(first_tile + CWcol(l, 2) + t, 1)],
                      bias=prm[:, ds(first_tile + CBcol(l) + t, 1)]).then_inc(conv_act, 1)

            def mlp(l):
                q, g, gi = QUAD_FFN[l], G_FFN[l], 11 * l
                for g0, n in BLOCKS:
                    with act.Fori(0, n) as i:
                        for half in range(2):
                            for ks in range(4):
                                j = 4 * half + ks
                                split(q + 2 * i, j + 2)
                                if ks == 3:
                                    conv_last_tap(l, 8 * q + 16 * i + 8 * (half + 1), (ya, yg)[half],
                                                  4 * i + (4 * g0 + FT * half), half, 2 * i + 2 * (gi + g0))
                        for b in range(2):
                            act.wait_ge((bank0_free, bank1_free)[b], g + 2 * i + 2)
                            A(yg[:, 2 * b:2 * b + 2, :], yg[:, 2 * b:2 * b + 2, :], ACT.Silu).then_inc(silu_done, 1)
                        for b in range(2):
                            act.wait_ge(gg_ready, 2 * i + 2 * (gi + g0) + b + 1)
                            A(g_hi[:, ds(4 * i + 2 * b, 2), :], yg[:, 2 * b:2 * b + 2, :],
                              ACT.Copy).then_inc(ghi_ready, 1)
                    q += 2 * n
                    g += 2 * n
                    if n == 4:
                        with act.Fori(0, 2) as i:
                            for j in range(8):
                                split(q + 2 * i, j + 2)
                        q += 4
                        g += 4
                    else:
                        for u in range(12):
                            if 4 * q + u + 2 < UNITS:
                                split(q + (u + 2) // 4, (u + 2) % 4)
                            if u % 3 == 2:
                                squares(2 * l + 2, u // 3)

            root(1)
            modulate(1)
            mlp(0)
            root(2)
            act.wait_ge(mod_ready, 24 + 4)
            for gr in range(4):
                if gr:
                    act.wait_ge(pool_step, POOL_END[gr - 1])
                for t in range(4):
                    k = 4 * gr + t
                    act.wait_ge(t_ready, 2 * KT + k + 1)
                    A(hp[:, t, :], tmpn[:, t, :], ACT.Identity,
                      bias=mods[:, 96 + SH1 + k:96 + SH1 + k + 1]).then_inc(hp_ready, 1)
                act.wait_ge(pool_step, POOL_END[gr])
                A(h_hi[:, 4 * gr:4 * gr + 4, :], sA[:, :, :], ACT.Copy).then_inc(hhi_ready, 4)
            for u in range(4):
                split(QUAD_POOL + (u + 2) // 4, (u + 2) % 4)
                squares(3, u)
            root(3)
            modulate(3)
            mlp(1)
            root(4)
            for b in range(8):
                act.wait_ge(y_t, b + 1)
                A(o_tok[:, b // 4, 512 * (b % 4):512 * (b % 4) + 512], ps[:, b % 4, :], ACT.Copy).then_inc(y_cp, 1)

        @block.vector
        def _(dve):
            V = nc.vector
            steps = [0]

            def step(ins):
                ins.then_inc(dve_step, 1)
                steps[0] += 1
                dve.wait_ge(dve_step, steps[0])

            def split(q, j):
                for h in range(2):
                    dve.wait_ge(hi_ready, 8 * q + 2 * j + h + 1)
                    if not (isinstance(q, int) and 8 * q + 2 * j + h < 4):
                        dve.wait_ge(sub_used, 8 * q + 2 * j + h - 3)
                    s = (2 * j + h) % 4
                    V.tensor_tensor(w_lo[:, s, :, :],
                                    raw[:, j % 4, h * 1024:(h + 1) * 1024].rearrange("p (k n) -> p k n", k=2),
                                    w_hi[:, s, :, :].bitcast(F32), ALU.subtract).then_inc(lo_ready, 1)

            def piece(c_all, j, a, red):
                dve.wait_ge(mod_landed[j % 4], 32 * c_all + 16 * (j // 4 + 1))
                for kk in range(2):
                    k = 2 * j + kk
                    if k == 0:
                        if red is not None:
                            dve.wait_ge(mod_red, red)
                        V.tensor_scalar(macc[:, a, :], mraw[:, j % 4, kk, :], cond[:, 0:1], None,
                                        ALU.mult).then_inc(mod_acc, 1)
                    else:
                        dve.wait_ge(mod_acc, 16 * c_all + k)
                        V.scalar_tensor_tensor(macc[:, a, :], mraw[:, j % 4, kk, :], cond[:, k:k + 1],
                                               macc[:, a, :], ALU.mult, ALU.add).then_inc(mod_acc, 1)

            def mod_bias(c_all, l, c_l):
                dve.wait_ge(mod_red, c_all + 1)
                V.tensor_tensor(mods[:, ds(4 * c_all, 4)], ps[:, 7, 256:260],
                                prm[:, ds(P * (1 + l) + 4 * c_l, 4)], ALU.add).then_inc(mod_ready, 1)

            def norm_scale(n):
                dve.wait_ge(sum_done, 4 * n + 4)
                if n:
                    dve.wait_ge(t_ready, n * KT)
                V.tensor_scalar(rstd[:, :], ps[:, 6, 0:SEQ], 1.0 / D, EPS, ALU.mult, ALU.add).then_inc(ms_ready, 1)

            def norm_gain_vec(n):
                l, m = n // 2, n % 2
                dve.wait_ge(mod_ready, 24 * l + (20 if m else 8))
                sc = 96 * l + (SC2 if m else SC1)
                step(V.tensor_scalar(amul[:, n, :], mods[:, sc:sc + KT], 1.0, None, ALU.add))
                step(V.tensor_tensor(amul[:, n, :], amul[:, n, :],
                                     prm[:, GAIN + KT * n:GAIN + KT * (n + 1)], ALU.mult))

            def rstd_finish(n):
                dve.wait_ge(rt_ready, n + 1)
                step(V.reciprocal(rstd[:, :], rstd[:, :]))

            def scaled(n, t):
                V.scalar_tensor_tensor(tmpn[:, t % 4, :], xT[:, t, :], amul[:, n, t:t + 1], rstd[:, :],
                                       ALU.mult, ALU.mult).then_inc(t_ready, 1)

            def modulate(n):
                l, m = n // 2, n % 2
                sh = 96 * l + (SH2 if m else SH1)
                before = n * KT
                if n:
                    dve.wait_ge(bank1_free, XG[n] + 4)
                for t in range(KT + 2):
                    if t < KT:
                        if t >= 4:
                            dve.wait_ge(hhi_ready, before + t - 3)
                            dve.wait_ge(hlo_ready, before + t - 3)
                        scaled(n, t)
                    if t >= 2:
                        u = t - 2
                        dve.wait_ge(t_ready, n * KT + u + 1)
                        dve.wait_ge(hhi_ready, before + u + 1)
                        V.scalar_tensor_tensor(h_lo[:, u, :], tmpn[:, u % 4, :], mods[:, sh + u:sh + u + 1],
                                               h_hi[:, u, :].bitcast(F32), ALU.add,
                                               ALU.subtract).then_inc(hlo_ready, 1)

            def residual(g, used, slot, gate, tile0):
                dve.wait_ge(sub_used, used)
                dve.wait_ge(bank1_free, g)
                for t in range(4):
                    i = V.scalar_tensor_tensor(xT[:, ds(tile0 + t, 1), :].rearrange("p a n -> p (a n)"),
                                               bank_tile(slot, t), gate(tile0 + t),
                                               xT[:, ds(tile0 + t, 1), :].rearrange("p a n -> p (a n)"),
                                               ALU.mult, ALU.add)
                    if t % 2:
                        i.then_inc((bank0_free, bank1_free)[t // 2], 1)

            for b, (n0, n1) in enumerate(((0, 4), (4, 8), (8, 11))):
                dve.wait_ge(prm_t, b + 1)
                for k in range(n0, n1):
                    r = ([112, 96, 96] + [FT2] * 8)[k]
                    i = V.tensor_copy(prm[:, k * P:k * P + r], ps[:, 4 + b, (k - n0) * P:(k - n0) * P + r])
                i.then_inc(prm_ready, 1)
            for b in range(8):
                dve.wait_ge(x_t, b + 1)
                i = V.tensor_copy(xT[:, 2 * b:2 * b + 2, :].rearrange("p a n -> p (a n)"), ps[:, b % 4, :])
                i.then_inc(x_copied, 1)
            dve.wait_ge(cond_s, 1)
            def startup_chunks(c_all, first):
                for a in (1, 0):
                    cc = c_all + (1 - a)
                    for j in range(8):
                        piece(cc, j, a, None if first else cc - 1)
                    mod_bias(cc, 0, cc)
            startup_chunks(0, True)
            with dve.Fori(1, 4) as i:
                startup_chunks(2 * i, False)
            norm_scale(0)
            dve.wait_ge(prm_ready, 3)
            norm_gain_vec(0)
            rstd_finish(0)
            dve.wait_ge(wf_hi_s, 1)
            V.tensor_tensor(wf_lo[:, :, :], wf[:, :, :], wf_hi[:, :, :].bitcast(F32),
                            ALU.subtract).then_inc(wf_split, 1)
            dve.wait_ge(x_copied, 8)
            split(0, 0)
            split(0, 1)
            modulate(0)

            def stick_softplus(n):
                spn = att[:, 2 + n % 2, :]
                dve.wait_ge(l_ready, n + 1)
                if n >= 2:
                    dve.wait_ge(cum_done, n - 1)
                step(V.scalar_tensor_tensor(spn, att_bank(("z", n)), 0.0, att[:, n % 2, :], ALU.max, ALU.add))
                V.tensor_tensor(spn, spn, keep[:, :], ALU.mult).then_inc(sp_ready, 1)

            def stick_exponent(n):
                dve.wait_ge(cum_done, n + 1)
                if n >= 2:
                    dve.wait_ge(o_done, n - 1)
                V.scalar_tensor_tensor(weights_buf(n), att_bank(("z", n)), 0.0, drop[:, :],
                                       ALU.min, ALU.add).then_inc(att_free, 1)

            def softmax_bias(n):
                f = n - NSB
                pb = att[:, f % 4, :]
                dve.wait_ge(z_done, n + 1)
                if f >= 4:
                    dve.wait_ge(cum_done, n - 3)
                elif f >= 2:
                    dve.wait_ge(cum_done, NSB)
                V.tensor_tensor(pb, att_bank(("z", n)), dropf[:, :], ALU.add).then_inc(att_free, 1)
                dve.wait_ge(att_free, ALLOC[("z", n)] + 1)
                V.reduce_max(fst[:, 0, f, 0:1], pb[:, 0:P], AX_X)
                step(V.reduce_max(fst[:, 0, f, 1:2], pb[:, P:384], AX_X))
                step(V.tensor_tensor(fst[:, 1, f, :], fst[:, 0, f, :], Fq[:, f, :], ALU.add))
                V.tensor_tensor(fst[:, 2, f, :], Fq[:, f, :], fst[:, 1, f, :],
                                ALU.subtract).then_inc(bias_ready, 1)

            def softmax_scale(n):
                f = n - NSB
                pb = att[:, f % 4, :]
                dve.wait_ge(p_exp, 2 * f + 2)
                step(V.reciprocal(fst[:, 4, f, :], fst[:, 3, f, :]))
                V.tensor_scalar(pb[:, 0:P], pb[:, 0:P], fst[:, 4, f, 0:1], None, ALU.mult)
                V.tensor_scalar(pb[:, P:384], pb[:, P:384], fst[:, 4, f, 1:2], None,
                                ALU.mult).then_inc(p_ready, 1)

            def take_flipped(n):
                dve.wait_ge(cum_done, n + 1)
                dve.wait_ge(o_done, max(n - 3, NSB))
                V.tensor_copy(weights_buf(n), att_bank(("c", n))).then_inc(att_free, 1)

            def head_lo(n):
                dve.wait_ge(o_hi, n + 1)
                V.tensor_tensor(g_lo[:, n, :], out_bank(n), g_hi[:, n, :].bitcast(F32),
                                ALU.subtract).then_inc(o_lo, 1)

            def attention_steps(pos):
                if pos == 4:
                    dve.wait_ge(f_done, 1)
                    dve.wait_ge(s_wf, 32)
                    for a in range(QT):
                        i = V.scalar_tensor_tensor(fg[:, 0, a, :], ps[:, 6, a * NF:(a + 1) * NF], -1.0,
                                                   bfb[:, :], ALU.mult, ALU.subtract)
                    i.then_inc(f_dve, 1)
                if pos == 6:
                    dve.wait_ge(f_act, 3)
                    V.scalar_tensor_tensor(nls[:, :, :], fg[:, 0], 0.0, fg[:, 3],
                                           ALU.max, ALU.add).then_inc(f_dve, 1)
                if pos == 7:
                    dve.wait_ge(f_done, 2)
                    for a in range(QT):
                        i = V.tensor_scalar(Fq[:, :, a], ps[:, 6, a * NF:(a + 1) * NF], -1.0, None, ALU.mult)
                    i.then_inc(f_dve, 1)
                todo = SCHED.get(pos, [])
                for kind, n in todo:
                    if kind == "c" and n < NSB:
                        stick_exponent(n)
                for kind, n in todo:
                    if kind == "z" and n < NSB:
                        stick_softplus(n)
                    elif kind == "z":
                        softmax_bias(n)
                for kind, n in todo:
                    if kind == "c" and n >= NSB:
                        take_flipped(n)
                for kind, n in todo:
                    if kind == "z" and n >= NSB:
                        softmax_scale(n)
                    elif kind == "o":
                        head_lo(n)

            def gate_at(l, col):
                return lambda t: mods[:, ds(96 * l + col + t, 1)]

            for pos in range(64):
                split((pos + 2) // 4, (pos + 2) % 4)
                ch, js = mod_at(pos)
                for j in js:
                    piece(ch, j, (ch + 1) % 2, ch - 1)
                if pos == 12:
                    dve.wait_ge(f_dve, 3)
                attention_steps(pos)
                if mod_sum_at(pos) is not None:
                    mod_bias(mod_sum_at(pos), 0, mod_sum_at(pos))
                if pos < 48 and pos % 4 == 3:
                    g = pos // 4
                    hg, kind, _ks = qkv_unit(pos)
                    dst = {"k": kT, "q": qT, "v": vv}[kind].rearrange("p a b -> p (a b)")[:, 512:1024]
                    dve.wait_ge(sub_used, 8 * (g + 1))
                    if hg:
                        if kind == "v":
                            dve.wait_ge(o_done, 4 * hg)
                        else:
                            dve.wait_ge(z_done, 4 * hg)
                    src = ps[:, 2 * (g % 2) + 1, :]
                    if kind == "q":
                        i = V.tensor_scalar(dst, src, SCALE, None, ALU.mult)
                    else:
                        i = V.tensor_copy(dst, src)
                    i.then_inc(bank1_free, 1)
                n = pos - 48
                if n in (6, 7, 11, 15):
                    cg = {6: 0, 7: 1, 11: 2, 15: 3}[n]
                    if cg == 0:
                        dve.wait_ge(mod_ready, 12)
                    residual(G_OUT + cg, 2 * (pos + 1), cg % 2, gate_at(0, G1), 4 * cg)
            mod_bias(23, 0, 23)

            def conv_taps(l, dst, first_tile, slot, c0):
                for b in range(2):
                    dve.wait_ge(conv_act, c0 + 2 * b + 2)
                    for tap, sh in ((1, 1), (0, 2)):
                        for t in (2 * b, 2 * b + 1):
                            if tap == 0:
                                dve.wait_ge(conv_tap, c0 + t + 1)
                            i = V.scalar_tensor_tensor(
                                dst[:, t, sh:SEQ], bank_tile(slot, t)[:, 0:SEQ - sh],
                                prm[:, ds(first_tile + CWcol(l, tap) + t, 1)], dst[:, t, sh:SEQ],
                                ALU.mult, ALU.add)
                            if tap == 1:
                                i.then_inc(conv_tap, 1)
                    i.then_inc((bank0_free, bank1_free)[b], 1)

            def mlp(l):
                q, g, gi = QUAD_FFN[l], G_FFN[l], 11 * l
                ch = 24 if l == 0 else 44
                gate = gate_at(l, G2)
                for g0, n in BLOCKS:
                    with_mod = l == 0 or g0 == 0
                    last_block = n == 3
                    with dve.Fori(0, n) as i:
                        for half in range(2):
                            for ks in range(4):
                                j = 4 * half + ks
                                split(q + 2 * i, j + 2)
                                if with_mod and j in (0, 1, 3, 4):
                                    p0 = 2 * (0, 1, 3, 4).index(j)
                                    for p in (p0, p0 + 1):
                                        piece(i + ch, p, 0, i + ch)
                                if with_mod and j == 6:
                                    mod_bias(i + ch, 1, i + (ch - 24))
                                if ks == 3:
                                    conv_taps(l, (ya, yg)[half], 4 * i + (4 * g0 + FT * half), half,
                                              8 * i + (8 * (gi + g0) + 4 * half))
                        for b in range(2):
                            dve.wait_ge(silu_done, 2 * i + (2 * (gi + g0) + b + 1))
                            dve.wait_ge((bank0_free, bank1_free)[b], g + 2 * i + 1)
                            V.tensor_tensor(yg[:, 2 * b:2 * b + 2, :], yg[:, 2 * b:2 * b + 2, :],
                                            ya[:, 2 * b:2 * b + 2, :], ALU.mult).then_inc(gg_ready, 1)
                        for b in range(2):
                            dve.wait_ge(ghi_ready, 2 * i + (2 * (gi + g0) + b + 1))
                            V.tensor_tensor(g_lo[:, ds(4 * i + 2 * b, 2), :], yg[:, 2 * b:2 * b + 2, :],
                                            g_hi[:, ds(4 * i + 2 * b, 2), :].bitcast(F32),
                                            ALU.subtract).then_inc(glo_ready, 1)
                    q += 2 * n
                    g += 2 * n
                    if with_mod:
                        ch += n
                    if g0 == 0:
                        dve.wait_ge(mod_ready, 24 * (l + 1))
                    if not last_block:
                        with dve.Fori(0, 2) as i:
                            for j in range(8):
                                split(q + 2 * i, j + 2)
                                if l == 0 and j < 6:
                                    a = 1 if j < 3 else 0
                                    for p in ((0, 1, 2), (3, 4, 5), (6, 7))[j % 3]:
                                        piece(2 * i + (ch + (1 - a)), p, a, 2 * i + (ch - a))
                                if l == 0 and j in (4, 7):
                                    o = 0 if j == 4 else 1
                                    mod_bias(2 * i + (ch + o), 1, 2 * i + (ch + o - 24))
                                if j % 4 == 3:
                                    residual(g + 2 * i + j // 4, 8 * q + 16 * i + 2 * j + 2, j // 4, gate,
                                             8 * i + 4 * (j // 4))
                        q += 4
                        g += 4
                        if l == 0:
                            ch += 4
                    else:
                        for u in range(12):
                            if 4 * q + u + 2 < UNITS:
                                split(q + (u + 2) // 4, (u + 2) % 4)
                            if l == 0 and u < 4:
                                for p in (2 * u, 2 * u + 1):
                                    piece(ch, p, 0, ch)
                            if l == 0 and u == 5:
                                mod_bias(ch, 1, ch - 24)
                            if u % 3 == 2:
                                cg = u // 3
                                residual(g + cg, 8 * q + 2 * u + 2, cg % 2, gate, 4 * cg)

            norm_scale(1)
            norm_gain_vec(1)
            rstd_finish(1)
            modulate(1)
            mlp(0)
            norm_scale(2)
            norm_gain_vec(2)
            rstd_finish(2)
            dve.wait_ge(mod_ready, 24 + 12)
            step(V.tensor_tensor(gps[:, :], mods[:, 96 + G1:96 + G1 + KT], prm[:, PSC:PSC + KT], ALU.mult))
            psteps = [0]

            def pstep(ins):
                ins.then_inc(pool_step, 1)
                psteps[0] += 1
                dve.wait_ge(pool_step, psteps[0])
            dve.wait_ge(bank1_free, XG[2] + 4)
            for gr in range(4):
                w = 2 << gr
                for t in range(4):
                    if gr:
                        dve.wait_ge(hp_ready, 4 * (gr - 1) + t + 1)
                    scaled(2, 4 * gr + t)
                dve.wait_ge(hp_ready, 4 * gr + 4)
                if gr:
                    dve.wait_ge(hhi_ready, 2 * KT + 4 * gr)
                src, dst, other = hp, (sB if gr % 2 else sA), (sA if gr % 2 else sB)
                s = 1
                while s < w:
                    V.tensor_copy(dst[:, :, 0:s], src[:, :, 0:s])
                    pstep(V.tensor_tensor(dst[:, :, s:SEQ], src[:, :, s:SEQ], src[:, :, 0:SEQ - s], ALU.add))
                    src, dst, other = dst, other, dst
                    s *= 2
                fix = invw[:, 0:w - 1]
                for t in range(4):
                    i = V.tensor_tensor(sB[:, t, 0:w - 1], sA[:, t, 0:w - 1], fix, ALU.mult)
                pstep(i)
                V.scalar_tensor_tensor(sA[:, :, w - 1:SEQ], sA[:, :, w - 1:SEQ], 1.0 / w, hp[:, :, w - 1:SEQ],
                                       ALU.mult, ALU.subtract)
                pstep(V.tensor_tensor(sA[:, :, 0:w - 1], sB[:, :, 0:w - 1], hp[:, :, 0:w - 1], ALU.subtract))
                assert psteps[0] == POOL_END[gr]
                dve.wait_ge(hhi_ready, 2 * KT + 4 * gr + 4)
                V.tensor_tensor(h_lo[:, 4 * gr:4 * gr + 4, :], sA[:, :, :],
                                h_hi[:, 4 * gr:4 * gr + 4, :].bitcast(F32), ALU.subtract).then_inc(hlo_ready, 4)
                if gr < 3:
                    dve.wait_ge(hlo_ready, 2 * KT + 4 * gr + 4)
            for u in range(4):
                split(QUAD_POOL + (u + 2) // 4, (u + 2) % 4)
                residual(G_POOL + u, 8 * QUAD_POOL + 2 * u + 2, u % 2, lambda t: gps[:, t:t + 1], 4 * u)
            norm_scale(3)
            norm_gain_vec(3)
            rstd_finish(3)
            modulate(3)
            mlp(1)
            norm_scale(4)
            rstd_finish(4)
            dve.wait_ge(bank1_free, XG[4] + 4)
            for t in range(KT):
                V.scalar_tensor_tensor(xT[:, t, :], xT[:, t, :], prm[:, FGAIN + t:FGAIN + t + 1], rstd[:, :],
                                       ALU.mult, ALU.mult).then_inc(t_ready, 1)


POOL_END = [3, 7, 12, 18]


_INS = ["x", "c", "w_mod", "b_mod", "norm_gain", "w_attn_in", "b_forget", "w_attn_out", "w_pool",
        "pool_scale", "w_up", "conv_w", "conv_b", "w_down", "final_gain"]


def kernel(**inputs):
    import numpy as np
    import concourse.bacc as bacc
    from concourse import mybir as mb
    from concourse.bass_utils import run_bass_kernel_spmd

    nc = bacc.Bacc("TRN2", target_bir_lowering=False, num_devices=1)
    arrays, args = {}, []
    for name in _INS:
        a = np.ascontiguousarray(inputs[name])
        arrays[f"in_{name}"] = a
        args.append(nc.dram_tensor(f"in_{name}", a.shape, mb.dt.from_np(a.dtype), kind="ExternalInput").ap())
    shape = tuple(inputs["x"].shape)
    args.append(nc.dram_tensor("out_0", shape, mb.dt.from_np(np.dtype("float32")), kind="ExternalOutput").ap())
    decoder_trunk(nc, *args)
    r = run_bass_kernel_spmd(nc, [arrays], core_ids=[0])
    return r.results[0]["out_0"]
```

```python
from contextlib import ExitStack

import concourse.bass as bass
from concourse import mybir

ALU = mybir.AluOpType
ACT = mybir.ActivationFunctionType
F32 = mybir.dt.float32
F32R = mybir.dt.float32r
AX_X = mybir.AxisListType.X

P = 128
NEG = -1.0e30
EPS = 1e-6
ds = bass.ds


def decoder_trunk(nc, x, c, w_mod, b_mod, norm_gain, w_attn_in, b_forget, w_attn_out, w_pool,
                  pool_scale, w_up, conv_w, conv_b, w_down, final_gain, out):
    _, SEQ, D = x.shape
    LAYERS = w_mod.shape[0]
    F2 = w_up.shape[2]
    FF = F2 // 2
    NF = b_forget.shape[1]
    HD = 128
    QT = SEQ // P
    KT = D // P
    FT = FF // P
    FT2 = 2 * FT
    assert SEQ == 256 and D == 2048 and LAYERS == 2 and NF == 8 and FT == 44
    SCALE = float(HD) ** -0.5
    NH = D // HD
    NSB = NH - NF

    UNIT_K, UNIT_N = 4, 512
    Q_QKV, Q_OUT, Q_UP, Q_DOWN = 12, 4, 2 * FT // 4, FT // 4
    QUAD_OUT = Q_QKV
    QUAD_FFN = [Q_QKV + Q_OUT, Q_QKV + Q_OUT + Q_UP + Q_DOWN + 1]
    QUAD_POOL = QUAD_FFN[1] - 1
    QUADS = QUAD_FFN[1] + Q_UP + Q_DOWN
    UNITS = 4 * QUADS
    BLOCKS = [(0, 4), (4, 4), (8, 3)]
    G_OUT = Q_QKV
    G_FFN = [G_OUT + 4, G_OUT + 4 + 2 * 11 + 12 + 4]
    G_POOL = G_FFN[1] - 4

    XG = [0, G_OUT, G_FFN[0] + 30, G_POOL, G_FFN[1] + 30]

    CHUNKS = w_mod.shape[2] // 512
    SH1, SC1, G1, SH2, SC2, G2 = [16 * n for n in range(6)]

    with ExitStack() as ctx:
        def sb(name, shape, dt=F32):
            return ctx.enter_context(nc.sbuf_tensor(name, shape, dt))

        def sem(name):
            return ctx.enter_context(nc.semaphore(name))

        xT = sb("xT", [P, KT, SEQ])
        h_hi = sb("h_hi", [P, KT, SEQ], F32R)
        h_lo = sb("h_lo", [P, KT, SEQ], F32R)
        g_hi = sb("g_hi", [P, 16, SEQ], F32R)
        g_lo = sb("g_lo", [P, 16, SEQ], F32R)
        raw = sb("raw", [P, 4, UNIT_K * UNIT_N])
        w_hi = sb("w_hi", [P, 4, 2, UNIT_N], F32R)
        w_lo = sb("w_lo", [P, 4, 2, UNIT_N], F32R)
        mraw = sb("mraw", [P, 4, 2, 512])
        macc = sb("macc", [P, 2, 2, 512])
        prm = sb("prm", [P, 11 * P])
        mods = sb("mods", [P, LAYERS * 96])
        amul = sb("amul", [P, 2 * LAYERS, KT])
        gps = sb("gps", [P, KT])
        cond = sb("cond", [P, KT])
        rstd = sb("rstd", [P, SEQ])
        ident = sb("ident", [P, P])
        ones = sb("ones", [P, P])
        negones = sb("negones", [P, P])
        negtri = sb("negtri", [P, P])
        tri = sb("tri", [P, P])
        keep = sb("keep", [P, 384])
        drop = sb("drop", [P, 384])
        dropf = sb("dropf", [P, 384])
        pmat = sb("pmat", [P, 4, 384])
        work = sb("work", [P, 6144])
        wf = sb("wf", [P, KT, NF])
        wf_hi = sb("wf_hi", [P, KT, NF], F32R)
        wf_lo = sb("wf_lo", [P, KT, NF], F32R)
        bfb = sb("bfb", [P, NF])
        fg = sb("fg", [P, 4, QT, NF])
        nls = sb("nls", [P, QT, NF])
        Fq = sb("Fq", [P, NF, QT])
        fst = sb("fst", [P, 5, NF, QT])

        ps = ctx.enter_context(nc.psum_tensor("ps", [P, 8, 512], F32))

        x_tok = work[:, 0:4096].rearrange("p (a n) -> p a n", a=QT)
        prow = work[:, 4096:4096 + 11 * P]
        kT = work[:, 0:1024].rearrange("p (h t) -> p h t", h=4)
        qT = work[:, 1024:2048].rearrange("p (h t) -> p h t", h=4)
        vv = work[:, 2048:3072].rearrange("p (a n) -> p a n", a=QT)
        att = work[:, 3072:3072 + 8 * 384].rearrange("p (b n) -> p b n", b=8)
        ya = work[:, 0:1024].rearrange("p (t n) -> p t n", t=4)
        yg = work[:, 1024:2048].rearrange("p (t n) -> p t n", t=4)
        zs = work[:, 0:2048].rearrange("p (b a n) -> p b a n", b=2, a=QT)
        sq = work[:, 4096:6144].rearrange("p (b t n) -> p b t n", b=2, t=4)
        tmpn = work[:, 3072:4096].rearrange("p (t n) -> p t n", t=4)
        o_tok = raw[:, 0:2, :]
        CWcol = lambda l, i: (3 + 3 * l + i) * P
        CBcol = lambda l: (9 + l) * P
        GAIN, PSC, FGAIN = 16, 80, 96

        def bank_tile(g2, t):
            return ps[:, 2 * g2 + t // 2, (t % 2) * 256:(t % 2) * 256 + 256]

        def pool_tile(gr, t):
            return bank_tile(2 + gr % 2, t)

        ROWS = [112, 96, 96] + [FT2] * 8

        def added(n, q):
            return n in (1, 2, 4) and q < 3
        ADDED = {k: i + 1 for i, k in enumerate((n, q) for n in (1, 2, 4) for q in range(3))}

        s_c = sem("c_landed")
        s_prm = sem("prm_landed")
        s_x = sem("x_landed")
        s_wf = sem("wf_landed")
        raw_landed = [sem(f"raw_landed{n}") for n in range(4)]
        mod_landed = [sem(f"mod_landed{n}") for n in range(4)]
        consts = sem("consts")
        c_t = sem("c_transposed")
        prm_t = sem("prm_transposed")
        prm_ready = sem("prm_ready")
        x_t = sem("x_transposed")
        x_copied = sem("x_copied")
        cond_s = sem("cond_silu")
        hi_ready = sem("hi_ready")
        lo_ready = sem("lo_ready")
        sub_used = sem("sub_used")
        bank0_free = sem("bank0_free")
        bank1_free = sem("bank1_free")
        mod_acc = sem("mod_acc")
        mod_red = sem("mod_reduced")
        mod_ready = sem("mod_ready")
        sq_ready = sem("sq_ready")
        sq_half = sem("sq_half")
        sq_added = sem("sq_added")
        sum_done = sem("sum_done")
        ms_ready = sem("ms_ready")
        rt_ready = sem("rt_ready")
        t_ready = sem("t_ready")
        hhi_ready = sem("hhi_ready")
        hlo_ready = sem("hlo_ready")
        wf_split = sem("wf_split")
        wf_hi_s = sem("wf_hi")
        f_done = sem("f_done")
        f_act = sem("f_act")
        f_dve = sem("f_dve")
        z_done = sem("z_done")
        sb_act = sem("sb_act")
        l_ready = sem("l_ready")
        sp_ready = sem("sp_ready")
        cum_done = sem("cum_done")
        w_ready = sem("w_ready")
        bias_ready = sem("bias_ready")
        p_exp = sem("p_exp")
        p_ready = sem("p_ready")
        att_free = sem("att_free")
        o_done = sem("o_done")
        o_hi = sem("o_hi")
        o_lo = sem("o_lo")
        conv_act = sem("conv_act")
        conv_tap = sem("conv_tap")
        silu_done = sem("silu_done")
        gg_ready = sem("gg_ready")
        ghi_ready = sem("ghi_ready")
        glo_ready = sem("glo_ready")
        pool_y = sem("pool_y")
        pool_res = sem("pool_res")
        y_t = sem("y_transposed")
        y_cp = [sem("y_copied_act"), sem("y_copied_dve")]
        dve_step = sem("dve_step")
        s_out = sem("out_stored")

        SCHED = {}
        for hg in range(4):
            base = 12 * (hg + 1)
            if hg < 2:
                a, b, o = [0, 1, 2, 4], [2, 3, 4, 6], [4, 5, 6, 8]
            elif hg == 2:
                a, b, o = [0, 1, 2, 3], [2, 3, 4, 5], [4, 5, 6, 7]
            else:
                a, b, o = [0, 0, 1, 1], [2, 2, 3, 3], [4, 4, 5, 5]
            for n in range(4):
                for kind, at in (("z", a[n]), ("c", b[n]), ("o", o[n])):
                    SCHED.setdefault(base + at, []).append((kind, 4 * hg + n))
        ORDER = {"z": 0, "c": 1, "o": 2}
        for v in SCHED.values():
            v.sort(key=lambda s: (ORDER[s[0]], s[1]))
        ALLOC = {}
        for pos in sorted(SCHED):
            for kind, n in SCHED[pos]:
                if kind == "z" or (kind == "c" and n >= NSB):
                    ALLOC[(kind, n)] = len(ALLOC)

        def att_bank(key):
            return ps[:, 4 + ALLOC[key] % 3, 0:384]

        def out_bank(n):
            return ps[:, 4 if n in (13, 15) else 7, 0:256]
        assert ALLOC[("c", 13)] % 3 == 0

        def weights_buf(n):
            return att[:, 4 + (n % 2 if n < NSB else n % 4), :]

        def qkv_unit(pos):
            hg, j = divmod(pos, 12)
            return hg, "kqv"[j // 4], j % 4
        OUT_UNITS = [(0, 0), (0, 1), (0, 2), (1, 0), (1, 1), (1, 2), (0, 3), (1, 3)] + \
                    [(cg, ks) for cg in (2, 3) for ks in range(4)]

        def mod_at(pos):
            return 8 + pos // 4, [2 * (pos % 4), 2 * (pos % 4) + 1]

        MOD_SUM = {7: 8, 19: 11, 31: 14, 44: 17, 54: 20}
        MOD_SUM.update({4 * n + 5: 8 + n for n in range(15) if n % 3})
        assert sorted(MOD_SUM[p] for p in MOD_SUM) == [MOD_SUM[p] for p in sorted(MOD_SUM)]
        mod_sum_at = MOD_SUM.get

        def o_before(pos):
            return sum(1 for q in SCHED if q < pos for s in SCHED[q] if s[0] == "o")

        MODS = {pos: 8 + sum(1 for p in range(pos) if mod_sum_at(p) is not None) for pos in range(64)}

        C_IDENT, C_ONES = 2, 3
        C_MASKS = C_ONES + 6 + 2 + 6
        C_POOL = C_MASKS + sum(1 + (2 << gr) - 1 + 4 + 2 for gr in range(4))

        block = ctx.enter_context(nc.Block())

        @block.sync
        def _(sp):
            def rows(v):
                return v.rearrange("(r p) -> r p", p=P)
            sp.dma_start(prow[0:KT, 0:P], rows(c[0])).then_inc(s_c, 16)
            sp.dma_start(prow[PSC:PSC + KT, 0:P], rows(pool_scale[0])).then_inc(s_prm, 16)
            sp.dma_start(prow[FGAIN:FGAIN + KT, 0:P], rows(final_gain)).then_inc(s_prm, 16)
            sp.dma_start(prow[GAIN:GAIN + 64, 0:P],
                         norm_gain.rearrange("l a (r p) -> (l a r) p", p=P)).then_inc(s_prm, 16)
            for l in range(LAYERS):
                sp.dma_start(prow[0:96, (1 + l) * P:(2 + l) * P], rows(b_mod[l])).then_inc(s_prm, 16)
                for i in range(3):
                    sp.dma_start(prow[0:FT2, CWcol(l, i):CWcol(l, i) + P], rows(conv_w[l, i])).then_inc(s_prm, 16)
                sp.dma_start(prow[0:FT2, CBcol(l):CBcol(l) + P], rows(conv_b[l])).then_inc(s_prm, 16)
            sp.dma_start(x_tok, x[0].rearrange("(a p) n -> p a n", p=P)).then_inc(s_x, 16)
            with nc.allow_non_contiguous_dma("the eight forget columns, the bias on every partition"):
                sp.dma_start(wf[:, :, :], w_attn_in[0, :, 3 * D:3 * D + NF]
                             .rearrange("(k p) n -> p k n", p=P)).then_inc(s_wf, 16)
                sp.dma_start(bfb[:, :], b_forget[0:1, :].to_broadcast([P, NF])).then_inc(s_wf, 16)
            sp.wait_ge(mod_acc, 16 * 6)

            def load(q, j, src):
                if not (isinstance(q, int) and q == 0):
                    sp.wait_ge(lo_ready, 8 * q + 2 * j - 6)
                sp.dma_start(raw[:, j % 4, :].rearrange("p (k n) -> p k n", k=UNIT_K),
                             src.rearrange("(k p) n -> p k n", p=P)).then_inc(raw_landed[j % 4], 16)

            for pos in range(48):
                hg, kind, ks = qkv_unit(pos)
                col = {"q": 0, "k": D, "v": 2 * D}[kind] + 512 * hg
                load(pos // 4, pos % 4, w_attn_in[0, 512 * ks:512 * ks + 512, col:col + 512])
            for n, (cg, ks) in enumerate(OUT_UNITS):
                load(QUAD_OUT + n // 4, n % 4,
                     w_attn_out[0, 512 * ks:512 * ks + 512, 512 * cg:512 * cg + 512])
            for l in range(LAYERS):
                if l == 1:
                    for g in range(4):
                        load(QUAD_POOL, g, w_pool[0, g])
                q = QUAD_FFN[l]
                for g0, n in BLOCKS:
                    with sp.Fori(0, n) as i:
                        for half in range(2):
                            for ks in range(4):
                                load(q + 2 * i + half, ks,
                                     w_up[l, 512 * ks:512 * ks + 512, ds(half * FF + 512 * g0 + 512 * i, 512)])
                    q += 2 * n
                    if n == 4:
                        with sp.Fori(0, 4) as i:
                            for ks in range(4):
                                load(q + i, ks, w_down[l, 512 * (g0 + ks):512 * (g0 + ks) + 512, ds(512 * i, 512)])
                        q += 4
                    else:
                        for cg in range(4):
                            for ks in range(3):
                                u = 3 * cg + ks
                                load(q + u // 4, u % 4,
                                     w_down[l, 512 * (g0 + ks):512 * (g0 + ks) + 512, 512 * cg:512 * cg + 512])
                        q += 3
            for b in range(8):
                k0, a = 4 * (b // 2), b % 2
                sp.wait_ge(y_cp[b % 2], b // 2 + 1)
                sp.dma_start(out[0, a * P:(a + 1) * P, k0 * P:(k0 + 4) * P],
                             o_tok[:, a, k0 * P:(k0 + 4) * P]).then_inc(s_out, 16)
            sp.wait_ge(s_out, 16 * 8)

        @block.gpsimd
        def _(pool):
            steps = [0]

            def const(ins):
                ins.then_inc(consts, 1)
                steps[0] += 1

            def select(t, cmp, fill, base, cm, step):
                pool.wait_ge(consts, steps[0])
                const(pool.affine_select(out=t, in_=t, compare_op=cmp, fill=fill, base=base,
                                         pattern=[[step, t.shape[-1]]], channel_multiplier=cm))

            def piece(l, c_all, c_l, j):
                if not (isinstance(c_all, int) and 8 * c_all + j < 4):
                    pool.wait_ge(mod_acc, 16 * c_all + 2 * j - 6)
                pool.dma_start(mraw[:, j % 4, :, :],
                               w_mod[l, 256 * j:256 * j + 256, ds(512 * c_l, 512)]
                               .rearrange("(k p) n -> p k n", p=P)).then_inc(mod_landed[j % 4], 16)

            def pieces(l, c0, c1):
                with pool.Fori(c0, c1) as i:
                    for j in range(8):
                        piece(l, i + l * CHUNKS, i, j)

            const(pool.memset(ident[:, :], 0.0))
            select(ident[:, :], ALU.not_equal, 1.0, 0, 1, -1)
            assert steps[0] == C_IDENT
            for j in range(4):
                piece(0, 0, 0, j)
            const(pool.memset(ones[:, :], 1.0))
            assert steps[0] == C_ONES
            for j in range(4, 8):
                piece(0, 0, 0, j)
            pieces(0, 1, 8)
            for t, v in ((negones, -1.0), (negtri, -1.0), (tri, 1.0), (keep, 1.0), (drop, 0.0), (dropf, 0.0)):
                const(pool.memset(t[:, :], v))
            select(negtri[:, :], ALU.is_ge, 0.0, 0, 1, -1)
            select(tri[:, :], ALU.is_ge, 0.0, 0, -1, 1)
            for c0 in (0, 256):
                select(keep[:, c0:c0 + P], ALU.is_gt, 0.0, 0, -1, 1)
                select(drop[:, c0:c0 + P], ALU.is_gt, NEG, 0, -1, 1)
                select(dropf[:, c0:c0 + P], ALU.is_ge, NEG, 0, 1, -1)
            assert steps[0] == C_MASKS
            pieces(0, 8, CHUNKS)
            for gr in range(4):
                w = 2 << gr
                const(pool.memset(pmat[:, gr, :], 1.0 / w))
                for t in range(w - 1):
                    pool.wait_ge(consts, steps[0])
                    const(pool.memset(pmat[:, gr, t:t + 1], 1.0 / (t + 1)))
                for c0, c1 in ((0, 256), (256, 384)):
                    select(pmat[:, gr, c0:c1], ALU.is_ge, 0.0, 0, -1, 1)
                    select(pmat[:, gr, c0:c1], ALU.is_ge, 0.0, w - 1, 1, -1)
                for c0 in (0, 256):
                    pool.wait_ge(consts, steps[0])
                    const(pool.tensor_tensor(pmat[:, gr, c0:c0 + P], pmat[:, gr, c0:c0 + P], ident[:, :],
                                             ALU.subtract))
            assert steps[0] == C_POOL
            pieces(1, 0, CHUNKS)

        @block.tensor
        def _(pe):
            mm = nc.tensor.matmul

            def sub(q, j, h, k, last_half, first, act_hi, act_lo, g2):
                pe.wait_ge(lo_ready, 8 * q + 2 * j + h + 1)
                s = (2 * j + h) % 4
                for kk in range(2):
                    for t in range(4):
                        o = bank_tile(g2, t)
                        wh, wl = (w[:, s, kk, t * P:(t + 1) * P] for w in (w_hi, w_lo))
                        ah, al = act_hi[:, k + kk, :], act_lo[:, k + kk, :]
                        st = first and kk == 0 and t % 2 == 0
                        mm(o, wh, ah, start=st, stop=False, skip_group_check=True)
                        mm(o, wh, al, start=False, stop=False, skip_group_check=True)
                        i = mm(o, wl, ah, start=False, stop=last_half and kk == 1, skip_group_check=True)
                i.then_inc(sub_used, 1)

            def unit(q, j, k0, first, last, act_hi, act_lo, g2, h_need=None):
                for h in range(2):
                    if h_need is not None:
                        pe.wait_ge(hlo_ready, h_need + k0 + 2 * h + 2)
                    sub(q, j, h, k0 + 2 * h, last and h == 1, first and h == 0, act_hi, act_lo, g2)

            def unit_tok(q, j, k0, first, last, g2):
                for h in range(2):
                    pe.wait_ge(lo_ready, 8 * q + 2 * j + h + 1)
                    s = (2 * j + h) % 4
                    for kk in range(2):
                        k = k0 + 2 * h + kk
                        for a in range(QT):
                            o = ps[:, 2 * g2 + a, :]
                            ah, al = (w[:, k, a * P:(a + 1) * P] for w in (h_hi, h_lo))
                            st = first and h == 0 and kk == 0
                            sp_ = last and h == 1 and kk == 1
                            mm(o, ah, w_hi[:, s, kk, :], start=st, stop=False)
                            mm(o, ah, w_lo[:, s, kk, :], start=False, stop=False)
                            i = mm(o, al, w_hi[:, s, kk, :], start=False, stop=sp_)
                    i.then_inc(sub_used, 1)

            def group_slot_free(g):
                pe.wait_ge(bank0_free, g - 1)
                pe.wait_ge(bank1_free, g - 1)

            def mod_sum(c_all, a, o_written):
                pe.wait_ge(mod_acc, 16 * c_all + 16)
                if not (isinstance(c_all, int) and c_all == 0):
                    pe.wait_ge(mod_ready, c_all)
                if o_written:
                    pe.wait_ge(o_lo, o_written)
                for t in range(4):
                    for odd in range(2):
                        i = mm(ps[:, 7, 256 + t:257 + t], macc[:, a, odd, t * P:(t + 1) * P], ones[:, 0:1],
                               start=odd == 0, stop=odd == 1)
                i.then_inc(mod_red, 1)

            def sum_squares(n, q):
                if added(n, q):
                    pe.wait_ge(sq_added, ADDED[(n, q)])
                else:
                    pe.wait_ge(sq_ready, 4 * n + q + 1)
                last = 1 if added(n, q) else 4
                for t in range(last):
                    i = mm(ps[:, 6, 0:SEQ], ones[:, :], sq[:, q % 2, t, :],
                           start=(q == 0 and t == 0), stop=(q == 3 and t == last - 1))
                i.then_inc(sum_done, 1)

            pe.wait_ge(consts, C_IDENT)
            pe.wait_ge(s_c, 16)
            nc.tensor.transpose(ps[:, 7, 0:KT], prow[0:KT, 0:P], ident[0:KT, 0:KT]).then_inc(c_t, 1)
            pe.wait_ge(s_prm, 16 * (3 + 5 * LAYERS))
            for b in range(11):
                i = nc.tensor.transpose(ps[:, 4 + b // 4, (b % 4) * P:(b % 4) * P + ROWS[b]],
                                        prow[0:ROWS[b], b * P:(b + 1) * P], ident[0:ROWS[b], 0:ROWS[b]])
                if b in (3, 7, 10):
                    i.then_inc(prm_t, 1)
            pe.wait_ge(s_x, 16)
            for b in range(8):
                if b >= 4:
                    pe.wait_ge(x_copied, b - 3)
                for t in range(2):
                    for a in range(QT):
                        k = 2 * b + t
                        i = nc.tensor.transpose(ps[:, b % 4, (2 * t + a) * P:(2 * t + a + 1) * P],
                                                x_tok[:, a, k * P:(k + 1) * P], ident[:, :])
                i.then_inc(x_t, 1)
            pe.wait_ge(prm_ready, 3)
            pe.wait_ge(consts, C_ONES)
            for q in range(4):
                sum_squares(0, q)
            pe.wait_ge(cond_s, 1)
            for ch in range(8):
                mod_sum(ch, (ch + 1) % 2, 0)

            def scores(n):
                pe.wait_ge(bank0_free, 3 * (n // 4 + 1))
                pe.wait_ge(bank1_free, 3 * (n // 4 + 1))
                if ALLOC[("z", n)] >= 3:
                    pe.wait_ge(att_free, ALLOC[("z", n)] - 2)
                z = att_bank(("z", n))
                k, q = kT[:, n % 4, :], qT[:, n % 4, :]
                if n < NSB:
                    mm(z[:, 0:256], k[:, 0:P], q, start=True, stop=False, skip_group_check=True)
                    i = mm(z[:, 256:384], k[:, P:2 * P], q[:, P:2 * P], start=False, stop=True, skip_group_check=True)
                else:
                    f = n - NSB
                    mm(z[:, 0:P], q[:, 0:P], k[:, 0:P], start=True, stop=False, skip_group_check=True)
                    mm(z[:, P:384], q[:, P:2 * P], k, start=False, stop=False, skip_group_check=True)
                    b0, b1 = (nls[:, a, f:f + 1].to_broadcast([P, P]) for a in range(QT))
                    mm(z[:, 0:P], b0, tri[:, :], start=False, stop=False, skip_group_check=True)
                    mm(z[:, P:2 * P], b0, tri[:, :], start=False, stop=False, skip_group_check=True)
                    mm(z[:, 2 * P:384], b0, ones[:, :], start=False, stop=False, skip_group_check=True)
                    i = mm(z[:, 2 * P:384], b1, tri[:, :], start=False, stop=True, skip_group_check=True)
                i.then_inc(z_done, 1)

            def suffix_sums(n):
                z = att_bank(("z", n))
                spn = att[:, 2 + n % 2, :]
                pe.wait_ge(sp_ready, n + 1)
                mm(z[:, 0:256], negtri[:, :], spn[:, 0:256], start=False, stop=False, skip_group_check=True)
                mm(z[:, P:256], negones[:, :], spn[:, 256:384], start=False, stop=False, skip_group_check=True)
                mm(z[:, 256:384], negtri[:, :], spn[:, 256:384], start=False, stop=True,
                   skip_group_check=True).then_inc(cum_done, 1)

            def flip_probs(n):
                f = n - NSB
                pe.wait_ge(p_ready, f + 1)
                pe.wait_ge(att_free, ALLOC[("c", n)] - 2)
                o = att_bank(("c", n))
                for b in range(3):
                    i = nc.tensor.transpose(o[:, b * P:(b + 1) * P], att[:, f % 4, b * P:(b + 1) * P], ident[:, :])
                i.then_inc(cum_done, 1)

            def head_out(n, mods_written):
                if n < NSB:
                    pe.wait_ge(w_ready, n + 1)
                else:
                    pe.wait_ge(att_free, ALLOC[("c", n)] + 1)
                if n >= 13:
                    pe.wait_ge(att_free, ALLOC[("c", 13)] + 1)
                    pe.wait_ge(o_lo, n - 1)
                elif n:
                    pe.wait_ge(o_lo, n)
                pe.wait_ge(mod_ready, mods_written)
                w = weights_buf(n)
                v0, v1 = (vv[:, a, (n % 4) * HD:(n % 4 + 1) * HD] for a in range(QT))
                mm(out_bank(n), v0, w[:, 0:256], start=True, stop=False)
                mm(out_bank(n)[:, P:256], v1, w[:, 256:384], start=False, stop=True).then_inc(o_done, 1)

            def forget_logits():
                pe.wait_ge(wf_split, 1)
                pe.wait_ge(hlo_ready, KT)
                for a in range(QT):
                    for k in range(KT):
                        ah, al = (w[:, k, a * P:(a + 1) * P] for w in (h_hi, h_lo))
                        o = ps[:, 6, a * NF:(a + 1) * NF]
                        mm(o, ah, wf_hi[:, k, :], start=(k == 0), stop=False)
                        mm(o, ah, wf_lo[:, k, :], start=False, stop=False)
                        i = mm(o, al, wf_hi[:, k, :], start=False, stop=(k == KT - 1))
                i.then_inc(f_done, 1)

            def forget_sums():
                pe.wait_ge(f_dve, 2)
                mm(ps[:, 6, 0:NF], tri[:, :], nls[:, 0, :], start=True, stop=True)
                mm(ps[:, 6, NF:2 * NF], ones[:, :], nls[:, 0, :], start=True, stop=False)
                mm(ps[:, 6, NF:2 * NF], tri[:, :], nls[:, 1, :], start=False, stop=True).then_inc(f_done, 1)

            def attention_steps(pos):
                if pos == 4:
                    forget_logits()
                if pos == 7:
                    pe.wait_ge(consts, C_MASKS)
                    forget_sums()
                if pos == 12:
                    pe.wait_ge(f_dve, 3)
                for kind, n in SCHED.get(pos, []):
                    if kind == "z":
                        scores(n)
                    elif kind == "c":
                        (suffix_sums if n < NSB else flip_probs)(n)
                    else:
                        head_out(n, MODS[pos])
                if mod_sum_at(pos) is not None:
                    ch = mod_sum_at(pos)
                    mod_sum(ch, (ch + 1) % 2, o_before(pos))

            for pos in range(48):
                attention_steps(pos)
                hg, kind, ks = qkv_unit(pos)
                g = pos // 4
                if ks == 0 and g >= 2:
                    group_slot_free(g)
                if kind == "v":
                    unit_tok(pos // 4, pos % 4, 4 * ks, ks == 0, ks == 3, g % 2)
                else:
                    unit(pos // 4, pos % 4, 4 * ks, ks == 0, ks == 3, h_hi, h_lo, g % 2,
                         h_need=0 if pos < 4 else None)
            for n, (cg, ks) in enumerate(OUT_UNITS):
                pos = 48 + n
                attention_steps(pos)
                if n == 9:
                    sum_squares(1, 0)
                if n == 10:
                    sum_squares(1, 1)
                if n == 14:
                    sum_squares(1, 2)
                if ks == 0:
                    group_slot_free(G_OUT + cg)
                pe.wait_ge(o_lo, 4 * (ks + 1))
                unit(QUAD_OUT + n // 4, n % 4, 4 * ks, ks == 0, ks == 3, g_hi, g_lo, cg % 2)
            mod_sum(8 + 15, 0, NH)
            sum_squares(1, 3)

            def mlp(l):
                q, g, nrm = QUAD_FFN[l], G_FFN[l], 2 * l + 1
                ch = 24 if l == 0 else 44
                gi = 11 * l
                for g0, n in BLOCKS:
                    last_block = n == 3
                    with_mod = l == 0 or g0 == 0
                    with pe.Fori(0, n) as i:
                        for half in range(2):
                            group_slot_free(g + 2 * i + half)
                            for ks in range(4):
                                unit(q + 2 * i + half, ks, 4 * ks, ks == 0, ks == 3, h_hi, h_lo, half,
                                     h_need=KT * nrm)
                        if with_mod:
                            mod_sum(i + ch, 0, NH)
                    q += 2 * n
                    g += 2 * n
                    if with_mod:
                        ch += n
                    if not last_block:
                        with pe.Fori(0, 2) as i:
                            for half in range(2):
                                group_slot_free(g + 2 * i + half)
                                for ks in range(4):
                                    if l == 0 and half == 1 and ks == 0:
                                        mod_sum(2 * i + ch, 1, NH)
                                    pe.wait_ge(glo_ready, 2 * (gi + g0 + ks + 1))
                                    unit(q + 2 * i + half, ks, 4 * ks, ks == 0, ks == 3, g_hi, g_lo, half)
                            if l == 0:
                                mod_sum(2 * i + (ch + 1), 0, NH)
                        q += 4
                        g += 4
                        if l == 0:
                            ch += 4
                    else:
                        for cg in range(4):
                            group_slot_free(g + cg)
                            for ks in range(3):
                                u = 3 * cg + ks
                                if u in (5, 8, 11):
                                    sum_squares(2 * l + 2, (u - 5) // 3)
                                if l == 0 and u == 5:
                                    mod_sum(ch, 0, NH)
                                pe.wait_ge(glo_ready, 2 * (gi + g0 + ks + 1))
                                unit(q + u // 4, u % 4, 4 * ks, ks == 0, ks == 2, g_hi, g_lo, cg % 2)
                sum_squares(2 * l + 2, 3)

            mlp(0)
            def pool_project(gr):
                group_slot_free(G_POOL + gr)
                pe.wait_ge(hlo_ready, 2 * KT + 4 * gr + 4)
                unit_tok(QUAD_POOL, gr, 4 * gr, True, True, gr % 2)

            def pool_tokens(gr):
                pe.wait_ge(bank0_free, G_POOL + gr + 1)
                pe.wait_ge(bank1_free, G_POOL + gr + 1)
                if gr >= 2:
                    pe.wait_ge(pool_res, gr - 1)
                for t in range(4):
                    z0, z1 = (zs[:, gr % 2, a, t * P:(t + 1) * P] for a in range(QT))
                    o = pool_tile(gr, t)
                    mm(o[:, P:256], z1, pmat[:, gr, 256:384], start=t % 2 == 0, stop=False, skip_group_check=True)
                    i = mm(o, z0, pmat[:, gr, 0:256], start=False, stop=True, skip_group_check=True)
                i.then_inc(pool_y, 1)

            pe.wait_ge(consts, C_POOL)
            pe.wait_ge(mod_ready, 44)
            pool_project(0)
            pool_project(1)
            pool_tokens(0)
            pool_project(2)
            pool_tokens(1)
            pool_project(3)
            pool_tokens(2)
            pool_tokens(3)
            pe.wait_ge(pool_res, 4)
            for q in range(4):
                sum_squares(3, q)
            mlp(1)
            pe.wait_ge(bank1_free, G_FFN[1] + 34)
            for b in range(8):
                a, k0 = b % 2, 4 * (b // 2)
                pe.wait_ge(t_ready, 4 * KT + k0 + 4)
                if b >= 4:
                    pe.wait_ge(y_cp[b % 2], b // 2 - 1)
                for t in range(4):
                    i = nc.tensor.transpose(ps[:, b % 4, t * P:(t + 1) * P],
                                            xT[:, k0 + t, a * P:(a + 1) * P], ident[:, :])
                i.then_inc(y_t, 1)

        @block.scalar
        def _(act):
            def A(o, i, f, **kw):
                return nc.scalar.activation(o, i, f, **kw)

            def split(q, j):
                act.wait_ge(raw_landed[j % 4], 16 * (q + j // 4 + 1))
                for h in range(2):
                    if not (isinstance(q, int) and 8 * q + 2 * j + h < 4):
                        act.wait_ge(sub_used, 8 * q + 2 * j + h - 3)
                    A(w_hi[:, (2 * j + h) % 4, :, :],
                      raw[:, j % 4, h * 1024:(h + 1) * 1024].rearrange("p (k n) -> p k n", k=2),
                      ACT.Copy).then_inc(hi_ready, 1)

            def squares(n, q):
                if n == 0:
                    act.wait_ge(x_copied, 2 * (q + 1))
                elif n == 3:
                    act.wait_ge(pool_res, q + 1)
                else:
                    act.wait_ge(bank1_free, XG[n] + q + 1)
                if 4 * n + q >= 2:
                    act.wait_ge(sum_done, 4 * n + q - 1)
                A(sq[:, q % 2, :, :], xT[:, 4 * q:4 * q + 4, :], ACT.Square).then_inc(sq_ready, 1)

            def root(n):
                act.wait_ge(ms_ready, n + 1)
                A(rstd[:, :], rstd[:, :], ACT.Sqrt).then_inc(rt_ready, 1)

            def modulate(n):
                l, m = n // 2, n % 2
                sh = 96 * l + (SH2 if m else SH1)
                act.wait_ge(mod_ready, 24 * l + (16 if m else 4))
                for t in range(KT):
                    act.wait_ge(t_ready, n * KT + t + 1)
                    A(h_hi[:, t, :], tmpn[:, t % 4, :], ACT.Identity,
                      bias=mods[:, sh + t:sh + t + 1]).then_inc(hhi_ready, 1)

            act.wait_ge(c_t, 1)
            A(cond[:, :], ps[:, 7, 0:KT], ACT.Silu).then_inc(cond_s, 1)
            for b, (n0, n1) in enumerate(((0, 4), (4, 8), (8, 11))):
                act.wait_ge(prm_t, b + 1)
                for k in range(n0, n1):
                    i = A(prm[:, k * P:k * P + ROWS[k]], ps[:, 4 + b, (k - n0) * P:(k - n0) * P + ROWS[k]],
                          ACT.Copy)
                i.then_inc(prm_ready, 1)
            for b in range(8):
                act.wait_ge(x_t, b + 1)
                A(xT[:, 2 * b:2 * b + 2, :].rearrange("p a n -> p (a n)"), ps[:, b % 4, :],
                  ACT.Copy).then_inc(x_copied, 1)
            for q in range(4):
                squares(0, q)
            root(0)
            act.wait_ge(s_wf, 32)
            A(wf_hi[:, :, :], wf[:, :, :], ACT.Copy).then_inc(wf_hi_s, 1)
            split(0, 0)
            split(0, 1)
            modulate(0)

            def softplus_tail(n):
                z, L = att_bank(("z", n)), att[:, n % 2, :]
                act.wait_ge(z_done, n + 1)
                if n >= 2:
                    act.wait_ge(sp_ready, n - 1)
                A(L, z, ACT.Abs).then_inc(sb_act, 1)
                act.wait_ge(sb_act, 2 * n + 1)
                A(L, L, ACT.Exp, scale=-1.0).then_inc(sb_act, 1)
                act.wait_ge(sb_act, 2 * n + 2)
                A(L, L, ACT.Ln, bias=1.0).then_inc(l_ready, 1)

            def softmax_exp(n):
                f = n - NSB
                act.wait_ge(bias_ready, f + 1)
                for a, (lo, hi) in enumerate(((0, P), (P, 384))):
                    A(att[:, f % 4, lo:hi], att[:, f % 4, lo:hi], ACT.Exp, bias=fst[:, 2, f, a:a + 1],
                      accum_out=fst[:, 3, f, a:a + 1]).then_inc(p_exp, 1)

            def stick_weights(n):
                act.wait_ge(att_free, ALLOC[("z", n)] + 1)
                A(weights_buf(n), weights_buf(n), ACT.Exp).then_inc(w_ready, 1)

            def head_hi(n):
                act.wait_ge(o_done, n + 1)
                A(g_hi[:, n, :], out_bank(n), ACT.Copy).then_inc(o_hi, 1)

            def attention_steps(pos):
                if pos == 5:
                    act.wait_ge(f_dve, 1)
                    A(fg[:, 1], fg[:, 0], ACT.Abs).then_inc(f_act, 1)
                    act.wait_ge(f_act, 1)
                    A(fg[:, 2], fg[:, 1], ACT.Exp, scale=-1.0).then_inc(f_act, 1)
                    act.wait_ge(f_act, 2)
                    A(fg[:, 3], fg[:, 2], ACT.Ln, bias=1.0).then_inc(f_act, 1)
                for kind, n in SCHED.get(pos, []):
                    if kind == "z":
                        (softplus_tail if n < NSB else softmax_exp)(n)
                    elif kind == "c" and n < NSB:
                        stick_weights(n)
                    elif kind == "o":
                        head_hi(n)

            for pos in range(64):
                attention_steps(pos)
                split((pos + 2) // 4, (pos + 2) % 4)
                if pos < 48 and pos % 4 == 3:
                    g = pos // 4
                    hg, kind, _ks = qkv_unit(pos)
                    dst = {"k": kT, "q": qT, "v": vv}[kind].rearrange("p a b -> p (a b)")[:, 0:512]
                    act.wait_ge(sub_used, 8 * (g + 1))
                    if hg:
                        if kind == "v":
                            act.wait_ge(o_done, 4 * hg)
                        else:
                            act.wait_ge(z_done, 4 * hg)
                    A(dst, ps[:, 2 * (g % 2), :], ACT.Copy,
                      scale=SCALE if kind == "q" else 1.0).then_inc(bank0_free, 1)
                n = pos - 48
                if n in (6, 7, 11, 15):
                    squares(1, {6: 0, 7: 1, 11: 2, 15: 3}[n])

            def conv_last_tap(l, used, dst, first_tile, slot, need):
                act.wait_ge(sub_used, used)
                act.wait_ge(gg_ready, need)
                for t in range(4):
                    A(dst[:, t, :], bank_tile(slot, t), ACT.Identity,
                      scale=prm[:, ds(first_tile + CWcol(l, 2) + t, 1)],
                      bias=prm[:, ds(first_tile + CBcol(l) + t, 1)]).then_inc(conv_act, 1)

            def mlp(l):
                q, g, gi = QUAD_FFN[l], G_FFN[l], 11 * l
                for g0, n in BLOCKS:
                    with act.Fori(0, n) as i:
                        for half in range(2):
                            for ks in range(4):
                                j = 4 * half + ks
                                split(q + 2 * i, j + 2)
                                if ks == 3:
                                    conv_last_tap(l, 8 * q + 16 * i + 8 * (half + 1), (ya, yg)[half],
                                                  4 * i + (4 * g0 + FT * half), half,
                                                  2 * i + (2 * (gi + g0) + 1))
                        for b in range(2):
                            act.wait_ge((bank0_free, bank1_free)[b], g + 2 * i + 2)
                            A(yg[:, 2 * b:2 * b + 2, :], yg[:, 2 * b:2 * b + 2, :], ACT.Silu).then_inc(silu_done, 1)
                        for b in range(2):
                            act.wait_ge(gg_ready, 2 * i + (2 * (gi + g0) + b + 2))
                            A(g_hi[:, ds(4 * i + 2 * b, 2), :], yg[:, 2 * b:2 * b + 2, :],
                              ACT.Copy).then_inc(ghi_ready, 1)
                    q += 2 * n
                    g += 2 * n
                    if n == 4:
                        with act.Fori(0, 2) as i:
                            for j in range(8):
                                split(q + 2 * i, j + 2)
                        q += 4
                        g += 4
                    else:
                        for u in range(12):
                            if 4 * q + u + 2 < UNITS:
                                split(q + (u + 2) // 4, (u + 2) % 4)
                            if u % 3 == 2:
                                squares(2 * l + 2, u // 3)

            root(1)
            modulate(1)
            mlp(0)
            root(2)
            modulate(2)
            for u in range(4):
                split(QUAD_POOL + (u + 2) // 4, (u + 2) % 4)
                act.wait_ge(sub_used, 8 * QUAD_POOL + 2 * u + 2)
                if u >= 2:
                    act.wait_ge(pool_y, u - 1)
                A(zs[:, u % 2, 0, :], ps[:, 2 * (u % 2), :], ACT.Copy).then_inc(bank0_free, 1)
            for q in range(4):
                squares(3, q)
            root(3)
            modulate(3)
            mlp(1)
            root(4)
            for b in range(0, 8, 2):
                act.wait_ge(y_t, b + 1)
                A(o_tok[:, 0, 256 * b:256 * b + 512], ps[:, b % 4, :], ACT.Copy).then_inc(y_cp[0], 1)

        @block.vector
        def _(dve):
            V = nc.vector
            steps = [0]

            def step(ins):
                ins.then_inc(dve_step, 1)
                steps[0] += 1
                dve.wait_ge(dve_step, steps[0])

            def split(q, j):
                for h in range(2):
                    dve.wait_ge(hi_ready, 8 * q + 2 * j + h + 1)
                    if not (isinstance(q, int) and 8 * q + 2 * j + h < 4):
                        dve.wait_ge(sub_used, 8 * q + 2 * j + h - 3)
                    s = (2 * j + h) % 4
                    V.tensor_tensor(w_lo[:, s, :, :],
                                    raw[:, j % 4, h * 1024:(h + 1) * 1024].rearrange("p (k n) -> p k n", k=2),
                                    w_hi[:, s, :, :].bitcast(F32), ALU.subtract).then_inc(lo_ready, 1)

            def piece(c_all, j, a, red):
                dve.wait_ge(mod_landed[j % 4], 32 * c_all + 16 * (j // 4 + 1))
                for kk in range(2):
                    k = 2 * j + kk
                    if k == 0 and red is not None:
                        dve.wait_ge(mod_red, red)
                    if k < 2:
                        V.tensor_scalar(macc[:, a, kk, :], mraw[:, j % 4, kk, :], cond[:, k:k + 1], None,
                                        ALU.mult).then_inc(mod_acc, 1)
                    else:
                        dve.wait_ge(mod_acc, 16 * c_all + (k - 1))
                        V.scalar_tensor_tensor(macc[:, a, kk, :], mraw[:, j % 4, kk, :], cond[:, k:k + 1],
                                               macc[:, a, kk, :], ALU.mult, ALU.add).then_inc(mod_acc, 1)

            def mod_bias(c_all, l, c_l):
                dve.wait_ge(mod_red, c_all + 1)
                V.tensor_tensor(mods[:, ds(4 * c_all, 4)], ps[:, 7, 256:260],
                                prm[:, ds(P * (1 + l) + 4 * c_l, 4)], ALU.add).then_inc(mod_ready, 1)

            def norm_scale(n):
                dve.wait_ge(sum_done, 4 * n + 4)
                if n:
                    dve.wait_ge(t_ready, n * KT)
                V.tensor_scalar(rstd[:, :], ps[:, 6, 0:SEQ], 1.0 / D, EPS, ALU.mult, ALU.add).then_inc(ms_ready, 1)

            def norm_gain_vec(n):
                l, m = n // 2, n % 2
                dve.wait_ge(mod_ready, 24 * l + (20 if m else 8))
                sc = 96 * l + (SC2 if m else SC1)
                step(V.tensor_scalar(amul[:, n, :], mods[:, sc:sc + KT], 1.0, None, ALU.add))
                step(V.tensor_tensor(amul[:, n, :], amul[:, n, :],
                                     prm[:, GAIN + KT * n:GAIN + KT * (n + 1)], ALU.mult))

            def rstd_finish(n):
                dve.wait_ge(rt_ready, n + 1)
                step(V.reciprocal(rstd[:, :], rstd[:, :]))

            def scaled(n, t):
                V.scalar_tensor_tensor(tmpn[:, t % 4, :], xT[:, t, :], amul[:, n, t:t + 1], rstd[:, :],
                                       ALU.mult, ALU.mult).then_inc(t_ready, 1)

            def modulate(n):
                l, m = n // 2, n % 2
                sh = 96 * l + (SH2 if m else SH1)
                before = n * KT
                if n == 3:
                    dve.wait_ge(pool_res, 4)
                elif n:
                    dve.wait_ge(bank1_free, XG[n] + 4)
                for t in range(KT + 2):
                    if t < KT:
                        if t >= 4:
                            dve.wait_ge(hhi_ready, before + t - 3)
                            dve.wait_ge(hlo_ready, before + t - 3)
                        scaled(n, t)
                    if t >= 2:
                        u = t - 2
                        dve.wait_ge(t_ready, n * KT + u + 1)
                        dve.wait_ge(hhi_ready, before + u + 1)
                        V.scalar_tensor_tensor(h_lo[:, u, :], tmpn[:, u % 4, :], mods[:, sh + u:sh + u + 1],
                                               h_hi[:, u, :].bitcast(F32), ALU.add,
                                               ALU.subtract).then_inc(hlo_ready, 1)

            def residual(g, used, slot, gate, tile0):
                dve.wait_ge(sub_used, used)
                dve.wait_ge(bank1_free, g)
                for t in range(4):
                    i = V.scalar_tensor_tensor(xT[:, ds(tile0 + t, 1), :].rearrange("p a n -> p (a n)"),
                                               bank_tile(slot, t), gate(tile0 + t),
                                               xT[:, ds(tile0 + t, 1), :].rearrange("p a n -> p (a n)"),
                                               ALU.mult, ALU.add)
                    if t % 2:
                        i.then_inc((bank0_free, bank1_free)[t // 2], 1)

            def add_squares(n, q):
                dve.wait_ge(sq_ready, 4 * n + q + 1)
                v = sq[:, q % 2]
                V.tensor_tensor(v[:, 0:2], v[:, 0:2], v[:, 2:4], ALU.add).then_inc(sq_half, 1)
                dve.wait_ge(sq_half, ADDED[(n, q)])
                V.tensor_tensor(v[:, 0], v[:, 0], v[:, 1], ALU.add).then_inc(sq_added, 1)

            dve.wait_ge(cond_s, 1)
            for ch in range(8):
                for j in range(8):
                    piece(ch, j, (ch + 1) % 2, ch - 1 if ch >= 2 else None)
                    if j == 2 and ch:
                        if ch == 1:
                            dve.wait_ge(prm_ready, 3)
                        mod_bias(ch - 1, 0, ch - 1)
            mod_bias(7, 0, 7)
            dve.wait_ge(x_copied, 8)
            norm_scale(0)
            norm_gain_vec(0)
            rstd_finish(0)
            dve.wait_ge(wf_hi_s, 1)
            V.tensor_tensor(wf_lo[:, :, :], wf[:, :, :], wf_hi[:, :, :].bitcast(F32),
                            ALU.subtract).then_inc(wf_split, 1)
            split(0, 0)
            split(0, 1)
            modulate(0)

            def stick_softplus(n):
                spn = att[:, 2 + n % 2, :]
                dve.wait_ge(l_ready, n + 1)
                if n >= 2:
                    dve.wait_ge(cum_done, n - 1)
                step(V.scalar_tensor_tensor(spn, att_bank(("z", n)), 0.0, att[:, n % 2, :], ALU.max, ALU.add))
                V.tensor_tensor(spn, spn, keep[:, :], ALU.mult).then_inc(sp_ready, 1)

            def stick_exponent(n):
                dve.wait_ge(cum_done, n + 1)
                if n >= 2:
                    dve.wait_ge(o_done, n - 1)
                V.scalar_tensor_tensor(weights_buf(n), att_bank(("z", n)), 0.0, drop[:, :],
                                       ALU.min, ALU.add).then_inc(att_free, 1)

            def softmax_bias(n):
                f = n - NSB
                pb = att[:, f % 4, :]
                dve.wait_ge(z_done, n + 1)
                if f >= 4:
                    dve.wait_ge(cum_done, n - 3)
                elif f >= 2:
                    dve.wait_ge(cum_done, NSB)
                V.tensor_tensor(pb, att_bank(("z", n)), dropf[:, :], ALU.add).then_inc(att_free, 1)
                dve.wait_ge(att_free, ALLOC[("z", n)] + 1)
                V.reduce_max(fst[:, 0, f, 0:1], pb[:, 0:P], AX_X)
                step(V.reduce_max(fst[:, 0, f, 1:2], pb[:, P:384], AX_X))
                step(V.tensor_tensor(fst[:, 1, f, :], fst[:, 0, f, :], Fq[:, f, :], ALU.add))
                V.tensor_tensor(fst[:, 2, f, :], Fq[:, f, :], fst[:, 1, f, :],
                                ALU.subtract).then_inc(bias_ready, 1)

            def softmax_scale(n):
                f = n - NSB
                pb = att[:, f % 4, :]
                dve.wait_ge(p_exp, 2 * f + 2)
                step(V.reciprocal(fst[:, 4, f, :], fst[:, 3, f, :]))
                V.tensor_scalar(pb[:, 0:P], pb[:, 0:P], fst[:, 4, f, 0:1], None, ALU.mult)
                V.tensor_scalar(pb[:, P:384], pb[:, P:384], fst[:, 4, f, 1:2], None,
                                ALU.mult).then_inc(p_ready, 1)

            def take_flipped(n):
                dve.wait_ge(cum_done, n + 1)
                dve.wait_ge(o_done, max(n - 3, NSB))
                V.tensor_copy(weights_buf(n), att_bank(("c", n))).then_inc(att_free, 1)

            def head_lo(n):
                dve.wait_ge(o_hi, n + 1)
                V.tensor_tensor(g_lo[:, n, :], out_bank(n), g_hi[:, n, :].bitcast(F32),
                                ALU.subtract).then_inc(o_lo, 1)

            def attention_steps(pos):
                if pos == 4:
                    dve.wait_ge(f_done, 1)
                    dve.wait_ge(s_wf, 32)
                    for a in range(QT):
                        i = V.scalar_tensor_tensor(fg[:, 0, a, :], ps[:, 6, a * NF:(a + 1) * NF], -1.0,
                                                   bfb[:, :], ALU.mult, ALU.subtract)
                    i.then_inc(f_dve, 1)
                if pos == 6:
                    dve.wait_ge(f_act, 3)
                    V.scalar_tensor_tensor(nls[:, :, :], fg[:, 0], 0.0, fg[:, 3],
                                           ALU.max, ALU.add).then_inc(f_dve, 1)
                if pos == 7:
                    dve.wait_ge(f_done, 2)
                    for a in range(QT):
                        i = V.tensor_scalar(Fq[:, :, a], ps[:, 6, a * NF:(a + 1) * NF], -1.0, None, ALU.mult)
                    i.then_inc(f_dve, 1)
                todo = SCHED.get(pos, [])
                for kind, n in todo:
                    if kind == "c" and n < NSB:
                        stick_exponent(n)
                for kind, n in todo:
                    if kind == "z" and n < NSB:
                        stick_softplus(n)
                    elif kind == "z":
                        softmax_bias(n)
                for kind, n in todo:
                    if kind == "c" and n >= NSB:
                        take_flipped(n)
                for kind, n in todo:
                    if kind == "z" and n >= NSB:
                        softmax_scale(n)
                    elif kind == "o":
                        head_lo(n)

            def gate_at(l, col):
                return lambda t: mods[:, ds(96 * l + col + t, 1)]

            dve.wait_ge(consts, C_MASKS)
            for pos in range(64):
                if pos == 12:
                    dve.wait_ge(f_dve, 3)
                attention_steps(pos)
                if mod_sum_at(pos) is not None:
                    mod_bias(mod_sum_at(pos), 0, mod_sum_at(pos))
                ch, js = mod_at(pos)
                for j in js:
                    piece(ch, j, (ch + 1) % 2, ch - 1)
                if pos - 48 in (7, 8, 12):
                    add_squares(1, {7: 0, 8: 1, 12: 2}[pos - 48])
                split((pos + 2) // 4, (pos + 2) % 4)
                if pos < 48 and pos % 4 == 3:
                    g = pos // 4
                    hg, kind, _ks = qkv_unit(pos)
                    dst = {"k": kT, "q": qT, "v": vv}[kind].rearrange("p a b -> p (a b)")[:, 512:1024]
                    dve.wait_ge(sub_used, 8 * (g + 1))
                    if hg:
                        if kind == "v":
                            dve.wait_ge(o_done, 4 * hg)
                        else:
                            dve.wait_ge(z_done, 4 * hg)
                    src = ps[:, 2 * (g % 2) + 1, :]
                    if kind == "q":
                        i = V.tensor_scalar(dst, src, SCALE, None, ALU.mult)
                    else:
                        i = V.tensor_copy(dst, src)
                    i.then_inc(bank1_free, 1)
                n = pos - 48
                if n in (6, 7, 11, 15):
                    cg = {6: 0, 7: 1, 11: 2, 15: 3}[n]
                    if cg == 0:
                        dve.wait_ge(mod_ready, 12)
                    residual(G_OUT + cg, 2 * (pos + 1), cg % 2, gate_at(0, G1), 4 * cg)
            mod_bias(23, 0, 23)

            def conv_taps(l, dst, first_tile, slot, c0):
                for b in range(2):
                    dve.wait_ge(conv_act, c0 + 2 * b + 2)
                    for tap, sh in ((1, 1), (0, 2)):
                        for t in (2 * b, 2 * b + 1):
                            if tap == 0:
                                dve.wait_ge(conv_tap, c0 + t + 1)
                            i = V.scalar_tensor_tensor(
                                dst[:, t, sh:SEQ], bank_tile(slot, t)[:, 0:SEQ - sh],
                                prm[:, ds(first_tile + CWcol(l, tap) + t, 1)], dst[:, t, sh:SEQ],
                                ALU.mult, ALU.add)
                            if tap == 1:
                                i.then_inc(conv_tap, 1)
                    i.then_inc((bank0_free, bank1_free)[b], 1)

            def mlp(l):
                q, g, gi = QUAD_FFN[l], G_FFN[l], 11 * l
                ch = 24 if l == 0 else 44
                gate = gate_at(l, G2)
                for g0, n in BLOCKS:
                    with_mod = l == 0 or g0 == 0
                    last_block = n == 3
                    with dve.Fori(0, n) as i:
                        for half in range(2):
                            for ks in range(4):
                                j = 4 * half + ks
                                if with_mod and j in (1, 2, 5, 6):
                                    p0 = 2 * (1, 2, 5, 6).index(j)
                                    for p in (p0, p0 + 1):
                                        piece(i + ch, p, 0, i + ch)
                                split(q + 2 * i, j + 2)
                                if ks == 3:
                                    conv_taps(l, (ya, yg)[half], 4 * i + (4 * g0 + FT * half), half,
                                              8 * i + (8 * (gi + g0) + 4 * half))
                        for b in range(2):
                            dve.wait_ge(silu_done, 2 * i + (2 * (gi + g0) + b + 1))
                            dve.wait_ge((bank0_free, bank1_free)[b], g + 2 * i + 1)
                            V.tensor_tensor(yg[:, 2 * b:2 * b + 2, :], yg[:, 2 * b:2 * b + 2, :],
                                            ya[:, 2 * b:2 * b + 2, :], ALU.mult).then_inc(gg_ready, 1)
                        for b in range(2):
                            dve.wait_ge(ghi_ready, 2 * i + (2 * (gi + g0) + b + 1))
                            V.tensor_tensor(g_lo[:, ds(4 * i + 2 * b, 2), :], yg[:, 2 * b:2 * b + 2, :],
                                            g_hi[:, ds(4 * i + 2 * b, 2), :].bitcast(F32),
                                            ALU.subtract).then_inc(glo_ready, 1)
                        if with_mod:
                            mod_bias(i + ch, 1, i + (ch - 24))
                    q += 2 * n
                    g += 2 * n
                    if with_mod:
                        ch += n
                    if g0 == 0:
                        dve.wait_ge(mod_ready, 24 * (l + 1))
                    if not last_block:
                        with dve.Fori(0, 2) as i:
                            for j in range(8):
                                if l == 0 and j == 4:
                                    mod_bias(2 * i + ch, 1, 2 * i + (ch - 24))
                                if l == 0 and j % 4 < 3:
                                    a = 1 if j < 4 else 0
                                    for p in ((0, 1, 2), (3, 4, 5), (6, 7))[j % 4]:
                                        piece(2 * i + (ch + (1 - a)), p, a, 2 * i + (ch - a))
                                split(q + 2 * i, j + 2)
                                if j % 4 == 3:
                                    residual(g + 2 * i + j // 4, 8 * q + 16 * i + 2 * j + 2, j // 4, gate,
                                             8 * i + 4 * (j // 4))
                                if l == 0 and j == 7:
                                    mod_bias(2 * i + (ch + 1), 1, 2 * i + (ch - 23))
                        q += 4
                        g += 4
                        if l == 0:
                            ch += 4
                    else:
                        for u in range(12):
                            if l == 0 and u == 5:
                                mod_bias(ch, 1, ch - 24)
                            if l == 0 and u < 4:
                                for p in (2 * u, 2 * u + 1):
                                    piece(ch, p, 0, ch)
                            if u in (3, 6, 9):
                                add_squares(2 * l + 2, u // 3 - 1)
                            if 4 * q + u + 2 < UNITS:
                                split(q + (u + 2) // 4, (u + 2) % 4)
                            if u % 3 == 2:
                                cg = u // 3
                                residual(g + cg, 8 * q + 2 * u + 2, cg % 2, gate, 4 * cg)

            norm_scale(1)
            norm_gain_vec(1)
            rstd_finish(1)
            modulate(1)
            dve.sem_inc(gg_ready, 1)
            mlp(0)
            norm_scale(2)
            norm_gain_vec(2)
            rstd_finish(2)
            dve.wait_ge(mod_ready, 24 + 12)
            step(V.tensor_tensor(gps[:, :], mods[:, 96 + G1:96 + G1 + KT], prm[:, PSC:PSC + KT], ALU.mult))
            modulate(2)

            def pool_residual(gr):
                dve.wait_ge(pool_y, gr + 1)
                for t in range(4):
                    k = 4 * gr + t
                    i = V.scalar_tensor_tensor(xT[:, k, :], pool_tile(gr, t), gps[:, k:k + 1], xT[:, k, :],
                                               ALU.mult, ALU.add)
                i.then_inc(pool_res, 1)

            for u in range(4):
                split(QUAD_POOL + (u + 2) // 4, (u + 2) % 4)
                dve.wait_ge(sub_used, 8 * QUAD_POOL + 2 * u + 2)
                if u >= 2:
                    dve.wait_ge(pool_y, u - 1)
                V.tensor_copy(zs[:, u % 2, 1, :], ps[:, 2 * (u % 2) + 1, :]).then_inc(bank1_free, 1)
                if u:
                    pool_residual(u - 1)
            pool_residual(3)
            norm_scale(3)
            norm_gain_vec(3)
            rstd_finish(3)
            modulate(3)
            mlp(1)
            norm_scale(4)
            rstd_finish(4)
            dve.wait_ge(bank1_free, XG[4] + 4)
            for t in range(KT):
                V.scalar_tensor_tensor(xT[:, t, :], xT[:, t, :], prm[:, FGAIN + t:FGAIN + t + 1], rstd[:, :],
                                       ALU.mult, ALU.mult).then_inc(t_ready, 1)
            for b in range(1, 8, 2):
                dve.wait_ge(y_t, b + 1)
                V.tensor_copy(o_tok[:, 1, 256 * (b - 1):256 * (b - 1) + 512], ps[:, b % 4, :]).then_inc(y_cp[1], 1)


_INS = ["x", "c", "w_mod", "b_mod", "norm_gain", "w_attn_in", "b_forget", "w_attn_out", "w_pool",
        "pool_scale", "w_up", "conv_w", "conv_b", "w_down", "final_gain"]


def kernel(**inputs):
    import numpy as np
    import concourse.bacc as bacc
    from concourse import mybir as mb
    from concourse.bass_utils import run_bass_kernel_spmd

    nc = bacc.Bacc("TRN2", target_bir_lowering=False, num_devices=1, dynamic_dma_scratch_size=8192)
    arrays, args = {}, []
    for name in _INS:
        a = np.ascontiguousarray(inputs[name])
        arrays[f"in_{name}"] = a
        args.append(nc.dram_tensor(f"in_{name}", a.shape, mb.dt.from_np(a.dtype), kind="ExternalInput").ap())
    shape = tuple(inputs["x"].shape)
    args.append(nc.dram_tensor("out_0", shape, mb.dt.from_np(np.dtype("float32")), kind="ExternalOutput").ap())
    decoder_trunk(nc, *args)
    r = run_bass_kernel_spmd(nc, [arrays], core_ids=[0])
    return r.results[0]["out_0"]
```

```python
from contextlib import ExitStack

import concourse.bass as bass
from concourse import mybir

ALU = mybir.AluOpType
ACT = mybir.ActivationFunctionType
F32 = mybir.dt.float32
F32R = mybir.dt.float32r
AX_X = mybir.AxisListType.X

P = 128
NEG = -1.0e30
EPS = 1e-6
ds = bass.ds


def decoder_trunk(nc, x, c, w_mod, b_mod, norm_gain, w_attn_in, b_forget, w_attn_out, w_pool,
                  pool_scale, w_up, conv_w, conv_b, w_down, final_gain, out):
    _, SEQ, D = x.shape
    LAYERS = w_mod.shape[0]
    F2 = w_up.shape[2]
    FF = F2 // 2
    NF = b_forget.shape[1]
    HD = 128
    QT = SEQ // P
    KT = D // P
    FT = FF // P
    FT2 = 2 * FT
    assert SEQ == 256 and D == 2048 and LAYERS == 2 and NF == 8 and FT == 44
    SCALE = float(HD) ** -0.5
    NH = D // HD
    NSB = NH - NF

    UNIT_K, UNIT_N = 4, 512
    Q_QKV, Q_OUT, Q_UP, Q_DOWN = 12, 4, 2 * FT // 4, FT // 4
    QUAD_OUT = Q_QKV
    QUAD_FFN = [Q_QKV + Q_OUT, Q_QKV + Q_OUT + Q_UP + Q_DOWN + 1]
    QUAD_POOL = QUAD_FFN[1] - 1
    QUADS = QUAD_FFN[1] + Q_UP + Q_DOWN
    UNITS = 4 * QUADS
    BLOCKS = [(0, 4), (4, 4), (8, 3)]
    G_OUT = Q_QKV
    G_FFN = [G_OUT + 4, G_OUT + 4 + 2 * 11 + 12 + 4]
    G_POOL = G_FFN[1] - 4

    XG = [0, G_OUT, G_FFN[0] + 30, G_POOL, G_FFN[1] + 30]

    CHUNKS = w_mod.shape[2] // 512
    SH1, SC1, G1, SH2, SC2, G2 = [16 * n for n in range(6)]

    with ExitStack() as ctx:
        def sb(name, shape, dt=F32):
            return ctx.enter_context(nc.sbuf_tensor(name, shape, dt))

        def sem(name):
            return ctx.enter_context(nc.semaphore(name))

        xT = sb("xT", [P, KT, SEQ])
        h_hi = sb("h_hi", [P, KT, SEQ], F32R)
        h_lo = sb("h_lo", [P, KT, SEQ], F32R)
        g_hi = sb("g_hi", [P, 16, SEQ], F32R)
        g_lo = sb("g_lo", [P, 16, SEQ], F32R)
        raw = sb("raw", [P, 4, UNIT_K * UNIT_N])
        w_hi = sb("w_hi", [P, 4, 2, UNIT_N], F32R)
        w_lo = sb("w_lo", [P, 4, 2, UNIT_N], F32R)
        mraw = sb("mraw", [P, 4, 2, 512])
        macc = sb("macc", [P, 2, 2, 512])
        prm = sb("prm", [P, 11 * P])
        mods = sb("mods", [P, LAYERS * 96])
        amul = sb("amul", [P, 2 * LAYERS, KT])
        gps = sb("gps", [P, KT])
        cond = sb("cond", [P, KT])
        rstd = sb("rstd", [P, SEQ])
        ident = sb("ident", [P, P])
        ones = sb("ones", [P, P])
        negones = sb("negones", [P, P])
        negtri = sb("negtri", [P, P])
        tri = sb("tri", [P, P])
        keep = sb("keep", [P, 384])
        drop = sb("drop", [P, 384])
        dropf = sb("dropf", [P, 384])
        pmat = sb("pmat", [P, 4, 384])
        work = sb("work", [P, 6144])
        wf = sb("wf", [P, KT, NF])
        wf_hi = sb("wf_hi", [P, KT, NF], F32R)
        wf_lo = sb("wf_lo", [P, KT, NF], F32R)
        bfb = sb("bfb", [P, NF])
        fg = sb("fg", [P, 4, QT, NF])
        nls = sb("nls", [P, QT, NF])
        Fq = sb("Fq", [P, NF, QT])
        fst = sb("fst", [P, 5, NF, QT])

        ps = ctx.enter_context(nc.psum_tensor("ps", [P, 8, 512], F32))

        x_tok = work[:, 0:4096].rearrange("p (a n) -> p a n", a=QT)
        prow = work[:, 4096:4096 + 11 * P]
        kT = work[:, 0:1024].rearrange("p (h t) -> p h t", h=4)
        qT = work[:, 1024:2048].rearrange("p (h t) -> p h t", h=4)
        vv = work[:, 2048:3072].rearrange("p (a n) -> p a n", a=QT)
        att = work[:, 3072:3072 + 8 * 384].rearrange("p (b n) -> p b n", b=8)
        ya = work[:, 0:1024].rearrange("p (t n) -> p t n", t=4)
        yg = work[:, 1024:2048].rearrange("p (t n) -> p t n", t=4)
        zs = work[:, 0:2048].rearrange("p (b a n) -> p b a n", b=2, a=QT)
        sq = work[:, 4096:6144].rearrange("p (b t n) -> p b t n", b=2, t=4)
        tmpn = work[:, 3072:4096].rearrange("p (t n) -> p t n", t=4)
        o_tok = raw[:, 0:2, :]
        CWcol = lambda l, i: (3 + 3 * l + i) * P
        CBcol = lambda l: (9 + l) * P
        GAIN, PSC, FGAIN = 16, 80, 96

        def mod_slot(c_all, j):
            if extra(c_all, j):
                return work[:, 1024 * (j - 5):1024 * (j - 4)].rearrange("p (k n) -> p k n", k=2)
            return mraw[:, j % 4]

        def extra(c_all, j):
            return isinstance(c_all, int) and 2 <= c_all < 8 and j >= 5

        def mod_landing(c_all, j):
            if isinstance(c_all, int) and c_all < 8:
                if extra(c_all, j):
                    return extra_landed[j - 5], 16 * (c_all - 1)
                if c_all >= 2 and 1 <= j < 4:
                    return mod_landed[j], 16 * c_all + 48
            elif j % 4:
                return mod_landed[j % 4], 32 * c_all + 16 * (j // 4) - 80
            return mod_landed[j % 4], 32 * c_all + 16 * (j // 4) + 16

        def bank_tile(g2, t):
            return ps[:, 2 * g2 + t // 2, (t % 2) * 256:(t % 2) * 256 + 256]

        def pool_tile(gr, t):
            return bank_tile(2 + gr % 2, t)

        ROWS = [112, 96, 96] + [FT2] * 8

        def added(n, q):
            return n in (1, 2, 4) and q < 3
        ADDED = {k: i + 1 for i, k in enumerate((n, q) for n in (1, 2, 4) for q in range(3))}

        SUM_BANK = (6, 6, 6, 0, 6)

        def sq_count(n, q, h=1):
            return (4 + 5 * (n - 1) if n else 0) + q + 1 + (h if n and q == 3 else 0)

        s_c = sem("c_landed")
        s_prm = sem("prm_landed")
        s_x = sem("x_landed")
        s_wf = sem("wf_landed")
        raw_landed = [sem(f"raw_landed{n}") for n in range(4)]
        mod_landed = [sem(f"mod_landed{n}") for n in range(4)]
        extra_landed = [sem(f"extra_landed{n}") for n in range(3)]
        consts = sem("consts")
        c_t = sem("c_transposed")
        prm_t = sem("prm_transposed")
        prm_ready = sem("prm_ready")
        x_t = sem("x_transposed")
        x_copied = sem("x_copied")
        cond_s = sem("cond_silu")
        hi_ready = sem("hi_ready")
        lo_ready = sem("lo_ready")
        sub_used = sem("sub_used")
        bank0_free = sem("bank0_free")
        bank1_free = sem("bank1_free")
        mod_first = sem("mod_first")
        mod_acc = sem("mod_acc")
        mod_added = sem("mod_added")
        mod_red = sem("mod_reduced")
        mod_ready = sem("mod_ready")
        sq_ready = sem("sq_ready")
        sq_half = sem("sq_half")
        sq_added = sem("sq_added")
        sum_done = sem("sum_done")
        ms_ready = sem("ms_ready")
        rt_ready = sem("rt_ready")
        t_ready = sem("t_ready")
        hhi_ready = sem("hhi_ready")
        hlo_ready = sem("hlo_ready")
        wf_split = sem("wf_split")
        wf_hi_s = sem("wf_hi")
        f_done = sem("f_done")
        f_act = sem("f_act")
        f_dve = sem("f_dve")
        z_done = sem("z_done")
        sb_act = sem("sb_act")
        l_ready = sem("l_ready")
        sp_ready = sem("sp_ready")
        cum_done = sem("cum_done")
        w_ready = sem("w_ready")
        bias_ready = sem("bias_ready")
        p_exp = sem("p_exp")
        rsum_ready = sem("rsum_ready")
        p_ready = sem("p_ready")
        att_free = sem("att_free")
        o_done = sem("o_done")
        o_hi = sem("o_hi")
        o_lo = sem("o_lo")
        conv_act = sem("conv_act")
        conv_tap = sem("conv_tap")
        silu_done = sem("silu_done")
        gg_ready = sem("gg_ready")
        ghi_ready = sem("ghi_ready")
        glo_ready = sem("glo_ready")
        pool_y = sem("pool_y")
        pool_res = sem("pool_res")
        y_t = sem("y_transposed")
        y_cp = [sem("y_copied_act"), sem("y_copied_dve")]
        dve_step = sem("dve_step")
        s_out = sem("out_stored")

        SCHED = {}
        for hg in range(4):
            base = 12 * (hg + 1)
            if hg < 2:
                a, b, o = [0, 1, 2, 4], [2, 3, 4, 6], [4, 5, 6, 8]
            elif hg == 2:
                a, b, o = [0, 1, 2, 3], [2, 3, 4, 5], [4, 5, 6, 7]
            else:
                a, b, o = [0, 0, 1, 1], [2, 2, 3, 3], [4, 4, 5, 5]
            for n in range(4):
                for kind, at in (("z", a[n]), ("c", b[n]), ("o", o[n])):
                    SCHED.setdefault(base + at, []).append((kind, 4 * hg + n))
        ORDER = {"z": 0, "c": 1, "o": 2}
        for v in SCHED.values():
            v.sort(key=lambda s: (ORDER[s[0]], s[1]))
        ALLOC = {}
        for pos in sorted(SCHED):
            for kind, n in SCHED[pos]:
                if kind == "z" or (kind == "c" and n >= NSB):
                    ALLOC[(kind, n)] = len(ALLOC)

        def att_bank(key):
            return ps[:, 4 + ALLOC[key] % 3, 0:384]

        def out_bank(n):
            return ps[:, 4 if n in (13, 15) else 7, 0:256]
        assert ALLOC[("c", 13)] % 3 == 0

        def weights_buf(n):
            return att[:, 4 + (n % 2 if n < NSB else n % 4), :]

        def qkv_unit(pos):
            hg, j = divmod(pos, 12)
            return (hg, "kqv"[j % 3], j // 3) if hg == 0 else (hg, "kqv"[j // 4], j % 4)

        def qkv_slot(g):
            return 2 if g == 2 else g % 2

        def qkv_done(pos):
            if pos < 12:
                return pos - 9 if pos >= 9 else None
            return pos // 4 if pos < 48 and pos % 4 == 3 else None
        OUT_UNITS = [(0, 0), (0, 1), (0, 2), (1, 0), (1, 1), (1, 2), (0, 3), (1, 3)] + \
                    [(cg, ks) for cg in (2, 3) for ks in range(4)]

        def first_chunk(s):
            return 4 * (s % 2) + s // 2
        MOD_END = 62
        POS0 = 9

        def mod_at(pos):
            lo, hi = (min(128 * (p - POS0) // (MOD_END - POS0), 128) for p in (pos, pos + 1))
            return [(8 + i // 8, i % 8) for i in range(lo, hi)]

        MOD_SUM = {}
        for pos in range(POS0, 64):
            for ch, j in mod_at(pos):
                if j == 7 and ch < 23:
                    MOD_SUM[next(at for at in (pos + 2, pos + 1, *range(pos + 3, 64)) if at not in MOD_SUM and
                                 not any(k == "o" and n not in (13, 15) for k, n in SCHED.get(at, [])))] = ch
        assert sorted(MOD_SUM[p] for p in MOD_SUM) == [MOD_SUM[p] for p in sorted(MOD_SUM)]
        mod_sum_at = MOD_SUM.get

        def o_before(pos):
            return sum(1 for q in SCHED if q < pos for s in SCHED[q] if s[0] == "o")

        MODS = {pos: 8 + sum(1 for p in range(pos) if mod_sum_at(p) is not None) for pos in range(64)}

        C_IDENT, C_ONES = 2, 3
        C_MASKS = C_ONES + 6 + 2 + 6
        C_POOL = C_MASKS + sum(1 + (2 << gr) - 1 + 4 + 2 for gr in range(4))

        block = ctx.enter_context(nc.Block())

        @block.sync
        def _(sp):
            def rows(v):
                return v.rearrange("(r p) -> r p", p=P)
            sp.dma_start(prow[0:KT, 0:P], rows(c[0])).then_inc(s_c, 16)
            sp.dma_start(prow[PSC:PSC + KT, 0:P], rows(pool_scale[0])).then_inc(s_prm, 16)
            sp.dma_start(prow[FGAIN:FGAIN + KT, 0:P], rows(final_gain)).then_inc(s_prm, 16)
            sp.dma_start(prow[GAIN:GAIN + 64, 0:P],
                         norm_gain.rearrange("l a (r p) -> (l a r) p", p=P)).then_inc(s_prm, 16)
            for l in range(LAYERS):
                sp.dma_start(prow[0:96, (1 + l) * P:(2 + l) * P], rows(b_mod[l])).then_inc(s_prm, 16)
                for i in range(3):
                    sp.dma_start(prow[0:FT2, CWcol(l, i):CWcol(l, i) + P], rows(conv_w[l, i])).then_inc(s_prm, 16)
                sp.dma_start(prow[0:FT2, CBcol(l):CBcol(l) + P], rows(conv_b[l])).then_inc(s_prm, 16)
            sp.dma_start(x_tok, x[0].rearrange("(a p) n -> p a n", p=P)).then_inc(s_x, 16)
            with nc.allow_non_contiguous_dma("the eight forget columns, the bias on every partition"):
                sp.dma_start(wf[:, :, :], w_attn_in[0, :, 3 * D:3 * D + NF]
                             .rearrange("(k p) n -> p k n", p=P)).then_inc(s_wf, 16)
                sp.dma_start(bfb[:, :], b_forget[0:1, :].to_broadcast([P, NF])).then_inc(s_wf, 16)
            sp.wait_ge(mod_acc, 26)

            def load(q, j, src):
                if not (isinstance(q, int) and q == 0):
                    sp.wait_ge(lo_ready, 8 * q + 2 * j - 6)
                sp.dma_start(raw[:, j % 4, :].rearrange("p (k n) -> p k n", k=UNIT_K),
                             src.rearrange("(k p) n -> p k n", p=P)).then_inc(raw_landed[j % 4], 16)

            for pos in range(48):
                hg, kind, ks = qkv_unit(pos)
                col = {"q": 0, "k": D, "v": 2 * D}[kind] + 512 * hg
                load(pos // 4, pos % 4, w_attn_in[0, 512 * ks:512 * ks + 512, col:col + 512])
            for n, (cg, ks) in enumerate(OUT_UNITS):
                load(QUAD_OUT + n // 4, n % 4,
                     w_attn_out[0, 512 * ks:512 * ks + 512, 512 * cg:512 * cg + 512])
            for l in range(LAYERS):
                if l == 1:
                    for g in range(4):
                        load(QUAD_POOL, g, w_pool[0, g])
                q = QUAD_FFN[l]
                for g0, n in BLOCKS:
                    with sp.Fori(0, n) as i:
                        for half in range(2):
                            for ks in range(4):
                                load(q + 2 * i + half, ks,
                                     w_up[l, 512 * ks:512 * ks + 512, ds(half * FF + 512 * g0 + 512 * i, 512)])
                    q += 2 * n
                    if n == 4:
                        with sp.Fori(0, 4) as i:
                            for ks in range(4):
                                load(q + i, ks, w_down[l, 512 * (g0 + ks):512 * (g0 + ks) + 512, ds(512 * i, 512)])
                        q += 4
                    else:
                        for cg in range(4):
                            for ks in range(3):
                                u = 3 * cg + ks
                                load(q + u // 4, u % 4,
                                     w_down[l, 512 * (g0 + ks):512 * (g0 + ks) + 512, 512 * cg:512 * cg + 512])
                        q += 3
            for b in range(8):
                k0, a = 4 * (b // 2), b % 2
                sp.wait_ge(y_cp[b % 2], b // 2 + 1)
                sp.dma_start(out[0, a * P:(a + 1) * P, k0 * P:(k0 + 4) * P],
                             o_tok[:, a, k0 * P:(k0 + 4) * P]).then_inc(s_out, 16)
            sp.wait_ge(s_out, 16 * 8)

        @block.gpsimd
        def _(pool):
            steps = [0]

            def const(ins):
                ins.then_inc(consts, 1)
                steps[0] += 1

            def select(t, cmp, fill, base, cm, step):
                pool.wait_ge(consts, steps[0])
                const(pool.affine_select(out=t, in_=t, compare_op=cmp, fill=fill, base=base,
                                         pattern=[[step, t.shape[-1]]], channel_multiplier=cm))

            def land(l, c_l, j, slot, landed):
                pool.dma_start(slot, w_mod[l, 256 * j:256 * j + 256, ds(512 * c_l, 512)]
                               .rearrange("(k p) n -> p k n", p=P)).then_inc(landed, 16)

            def early_piece(c_all, c_l, j):
                if isinstance(c_all, int) and c_all == 2 or j in (0, 4):
                    if j < 5:
                        piece(0, c_all, c_l, j)
                        return
                    pool.wait_ge(x_copied, 8)
                else:
                    pool.wait_ge(mod_acc, 14 * c_all + 2 * j - 14)
                land(0, c_l, j, mod_slot(2, j), extra_landed[j - 5] if j >= 5 else mod_landed[j])

            def piece(l, c_all, c_l, j):
                if j < 4:
                    if not (isinstance(c_all, int) and c_all == 0):
                        pool.wait_ge(mod_acc, 14 * c_all + 2 * j - 6)
                elif j == 4:
                    pool.wait_ge(mod_first, 2 * c_all + 2)
                else:
                    pool.wait_ge(mod_acc, 14 * c_all + 2 * j - 8)
                land(l, c_l, j, mraw[:, j % 4], mod_landed[j % 4])

            def pieces(l, c0, c1):
                with pool.Fori(c0, c1) as i:
                    for j in range(8):
                        piece(l, i + l * CHUNKS, i, j)

            const(pool.memset(ident[:, :], 0.0))
            select(ident[:, :], ALU.not_equal, 1.0, 0, 1, -1)
            assert steps[0] == C_IDENT
            for j in range(4):
                piece(0, 0, 0, j)
            const(pool.memset(ones[:, :], 1.0))
            assert steps[0] == C_ONES
            for j in range(4, 8):
                piece(0, 0, 0, j)
            for j in range(8):
                piece(0, 1, first_chunk(1), j)
            for ch in (2, 3):
                for j in range(8):
                    early_piece(ch, first_chunk(ch), j)
            with pool.Fori(2, 4) as i:
                for odd in range(2):
                    for j in range(8):
                        early_piece(2 * i + odd, i + 4 * odd, j)
            for t, v in ((negones, -1.0), (negtri, -1.0), (tri, 1.0), (keep, 1.0), (drop, 0.0), (dropf, 0.0)):
                const(pool.memset(t[:, :], v))
            select(negtri[:, :], ALU.is_ge, 0.0, 0, 1, -1)
            select(tri[:, :], ALU.is_ge, 0.0, 0, -1, 1)
            for c0 in (0, 256):
                select(keep[:, c0:c0 + P], ALU.is_gt, 0.0, 0, -1, 1)
                select(drop[:, c0:c0 + P], ALU.is_gt, NEG, 0, -1, 1)
                select(dropf[:, c0:c0 + P], ALU.is_ge, NEG, 0, 1, -1)
            assert steps[0] == C_MASKS
            pieces(0, 8, CHUNKS)
            for gr in range(4):
                w = 2 << gr
                const(pool.memset(pmat[:, gr, :], 1.0 / w))
                for t in range(w - 1):
                    pool.wait_ge(consts, steps[0])
                    const(pool.memset(pmat[:, gr, t:t + 1], 1.0 / (t + 1)))
                for c0, c1 in ((0, 256), (256, 384)):
                    select(pmat[:, gr, c0:c1], ALU.is_ge, 0.0, 0, -1, 1)
                    select(pmat[:, gr, c0:c1], ALU.is_ge, 0.0, w - 1, 1, -1)
                for c0 in (0, 256):
                    pool.wait_ge(consts, steps[0])
                    const(pool.tensor_tensor(pmat[:, gr, c0:c0 + P], pmat[:, gr, c0:c0 + P], ident[:, :],
                                             ALU.subtract))
            assert steps[0] == C_POOL
            pieces(1, 0, CHUNKS)

        @block.tensor
        def _(pe):
            mm = nc.tensor.matmul

            def sub(q, j, h, k, last_half, first, act_hi, act_lo, g2):
                pe.wait_ge(lo_ready, 8 * q + 2 * j + h + 1)
                s = (2 * j + h) % 4
                for kk in range(2):
                    for t in range(4):
                        o = bank_tile(g2, t)
                        wh, wl = (w[:, s, kk, t * P:(t + 1) * P] for w in (w_hi, w_lo))
                        ah, al = act_hi[:, k + kk, :], act_lo[:, k + kk, :]
                        st = first and kk == 0 and t % 2 == 0
                        mm(o, wh, ah, start=st, stop=False, skip_group_check=True)
                        mm(o, wh, al, start=False, stop=False, skip_group_check=True)
                        i = mm(o, wl, ah, start=False, stop=last_half and kk == 1, skip_group_check=True)
                i.then_inc(sub_used, 1)

            def unit(q, j, k0, first, last, act_hi, act_lo, g2, h_need=None):
                for h in range(2):
                    if h_need is not None:
                        pe.wait_ge(hlo_ready, h_need + k0 + 2 * h + 2)
                    sub(q, j, h, k0 + 2 * h, last and h == 1, first and h == 0, act_hi, act_lo, g2)

            def unit_tok(q, j, k0, first, last, g2, h_need=None):
                for h in range(2):
                    if h_need is not None:
                        pe.wait_ge(hlo_ready, h_need + k0 + 2 * h + 2)
                    pe.wait_ge(lo_ready, 8 * q + 2 * j + h + 1)
                    s = (2 * j + h) % 4
                    for kk in range(2):
                        k = k0 + 2 * h + kk
                        for a in range(QT):
                            o = ps[:, 2 * g2 + a, :]
                            ah, al = (w[:, k, a * P:(a + 1) * P] for w in (h_hi, h_lo))
                            st = first and h == 0 and kk == 0
                            sp_ = last and h == 1 and kk == 1
                            mm(o, ah, w_hi[:, s, kk, :], start=st, stop=False)
                            mm(o, ah, w_lo[:, s, kk, :], start=False, stop=False)
                            i = mm(o, al, w_hi[:, s, kk, :], start=False, stop=sp_)
                    i.then_inc(sub_used, 1)

            def group_slot_free(g):
                pe.wait_ge(bank0_free, g - 1)
                pe.wait_ge(bank1_free, g - 1)

            def mod_sum(c_all, a, o_written):
                pe.wait_ge(mod_added, c_all + 1)
                if not (isinstance(c_all, int) and c_all == 0):
                    pe.wait_ge(mod_ready, c_all)
                if o_written:
                    pe.wait_ge(o_lo, o_written)
                for t in range(4):
                    i = mm(ps[:, 7, 256 + t:257 + t], macc[:, a, 0, t * P:(t + 1) * P], ones[:, 0:1],
                           start=True, stop=True)
                i.then_inc(mod_red, 1)

            def sum_squares(n, q):
                if added(n, q):
                    pe.wait_ge(sq_added, ADDED[(n, q)])
                last = 1 if added(n, q) else 4
                for t in range(last):
                    if not added(n, q) and t % 2 == 0:
                        pe.wait_ge(sq_ready, sq_count(n, q, t // 2))
                    i = mm(ps[:, SUM_BANK[n], 0:SEQ], ones[:, :], sq[:, q % 2, t, :],
                           start=(q == 0 and t == 0), stop=(q == 3 and t == last - 1))
                i.then_inc(sum_done, 1)

            pe.wait_ge(consts, C_IDENT)
            pe.wait_ge(s_c, 16)
            nc.tensor.transpose(ps[:, 7, 0:KT], prow[0:KT, 0:P], ident[0:KT, 0:KT]).then_inc(c_t, 1)
            pe.wait_ge(s_prm, 16 * (3 + 5 * LAYERS))
            for b in range(11):
                i = nc.tensor.transpose(ps[:, 4 + b // 4, (b % 4) * P:(b % 4) * P + ROWS[b]],
                                        prow[0:ROWS[b], b * P:(b + 1) * P], ident[0:ROWS[b], 0:ROWS[b]])
                if b in (3, 7, 10):
                    i.then_inc(prm_t, 1)
            pe.wait_ge(s_x, 16)
            for b in range(8):
                if b >= 4:
                    pe.wait_ge(x_copied, b - 3)
                for t in range(2):
                    for a in range(QT):
                        k = 2 * b + t
                        i = nc.tensor.transpose(ps[:, b % 4, (2 * t + a) * P:(2 * t + a + 1) * P],
                                                x_tok[:, a, k * P:(k + 1) * P], ident[:, :])
                i.then_inc(x_t, 1)
            pe.wait_ge(prm_ready, 3)
            pe.wait_ge(consts, C_ONES)
            pe.wait_ge(cond_s, 1)
            mod_sum(0, 1, 0)
            for q in range(4):
                sum_squares(0, q)

            def scores(n):
                pe.wait_ge(bank1_free, 3 * (n // 4) + (2 if n >= 4 else 3))
                if ALLOC[("z", n)] >= 3:
                    pe.wait_ge(att_free, ALLOC[("z", n)] - 2)
                z = att_bank(("z", n))
                k, q = kT[:, n % 4, :], qT[:, n % 4, :]
                if n < NSB:
                    mm(z[:, 0:256], k[:, 0:P], q, start=True, stop=False, skip_group_check=True)
                    i = mm(z[:, 256:384], k[:, P:2 * P], q[:, P:2 * P], start=False, stop=True, skip_group_check=True)
                else:
                    f = n - NSB
                    mm(z[:, 0:P], q[:, 0:P], k[:, 0:P], start=True, stop=False, skip_group_check=True)
                    mm(z[:, P:384], q[:, P:2 * P], k, start=False, stop=False, skip_group_check=True)
                    b0, b1 = (nls[:, a, f:f + 1].to_broadcast([P, P]) for a in range(QT))
                    mm(z[:, 0:P], b0, tri[:, :], start=False, stop=False, skip_group_check=True)
                    mm(z[:, P:2 * P], b0, tri[:, :], start=False, stop=False, skip_group_check=True)
                    mm(z[:, 2 * P:384], b0, ones[:, :], start=False, stop=False, skip_group_check=True)
                    i = mm(z[:, 2 * P:384], b1, tri[:, :], start=False, stop=True, skip_group_check=True)
                i.then_inc(z_done, 1)

            def suffix_sums(n):
                z = att_bank(("z", n))
                spn = att[:, 2 + n % 2, :]
                pe.wait_ge(sp_ready, n + 1)
                mm(z[:, 0:256], negtri[:, :], spn[:, 0:256], start=False, stop=False, skip_group_check=True)
                mm(z[:, P:256], negones[:, :], spn[:, 256:384], start=False, stop=False, skip_group_check=True)
                mm(z[:, 256:384], negtri[:, :], spn[:, 256:384], start=False, stop=True,
                   skip_group_check=True).then_inc(cum_done, 1)

            def flip_probs(n):
                f = n - NSB
                pe.wait_ge(p_ready, f + 1)
                pe.wait_ge(att_free, ALLOC[("c", n)] - 2)
                o = att_bank(("c", n))
                for b in range(3):
                    i = nc.tensor.transpose(o[:, b * P:(b + 1) * P], att[:, f % 4, b * P:(b + 1) * P], ident[:, :])
                i.then_inc(cum_done, 1)

            def head_out(n, mods_written):
                if n < NSB:
                    pe.wait_ge(w_ready, n + 1)
                else:
                    pe.wait_ge(att_free, ALLOC[("c", n)] + 1)
                if n >= 13:
                    pe.wait_ge(att_free, ALLOC[("c", 13)] + 1)
                    pe.wait_ge(o_lo, n - 1)
                elif n:
                    pe.wait_ge(o_lo, n)
                pe.wait_ge(mod_ready, mods_written)
                pe.wait_ge(bank1_free, 3 * (n // 4) + 3)
                w = weights_buf(n)
                v0, v1 = (vv[:, a, (n % 4) * HD:(n % 4 + 1) * HD] for a in range(QT))
                mm(out_bank(n), v0, w[:, 0:256], start=True, stop=False)
                mm(out_bank(n)[:, P:256], v1, w[:, 256:384], start=False, stop=True).then_inc(o_done, 1)

            def forget_logits(cq):
                if cq == 0:
                    pe.wait_ge(wf_split, 1)
                    pe.wait_ge(ms_ready, 1)
                pe.wait_ge(hlo_ready, 4 * cq + 4)
                for a in range(QT):
                    for k in range(4 * cq, 4 * cq + 4):
                        ah, al = (w[:, k, a * P:(a + 1) * P] for w in (h_hi, h_lo))
                        o = ps[:, 6, a * NF:(a + 1) * NF]
                        mm(o, ah, wf_hi[:, k, :], start=(k == 0 and a == 0), stop=False, skip_group_check=True)
                        mm(o, ah, wf_lo[:, k, :], start=False, stop=False, skip_group_check=True)
                        i = mm(o, al, wf_hi[:, k, :], start=False, stop=(k == KT - 1), skip_group_check=True)
                if cq == 3:
                    i.then_inc(f_done, 1)

            def forget_sums():
                pe.wait_ge(f_dve, 2)
                mm(ps[:, 6, 0:NF], tri[:, :], nls[:, 0, :], start=True, stop=True)
                mm(ps[:, 6, NF:2 * NF], ones[:, :], nls[:, 0, :], start=True, stop=False)
                mm(ps[:, 6, NF:2 * NF], tri[:, :], nls[:, 1, :], start=False, stop=True).then_inc(f_done, 1)

            def attention_steps(pos):
                if pos == 13:
                    forget_sums()
                if pos == 14:
                    pe.wait_ge(f_dve, 3)
                for kind, n in SCHED.get(pos, []):
                    if kind == "z":
                        scores(n)
                    elif kind == "c":
                        (suffix_sums if n < NSB else flip_probs)(n)
                    else:
                        head_out(n, MODS[pos])
                if mod_sum_at(pos) is not None:
                    ch = mod_sum_at(pos)
                    mod_sum(ch, (ch + 1) % 2, o_before(pos))

            def qkv_product(pos):
                hg, kind, ks = qkv_unit(pos)
                g = 3 * hg + "kqv".index(kind)
                if ks == 0 and g >= 3:
                    group_slot_free(g)
                if kind == "v":
                    unit_tok(pos // 4, pos % 4, 4 * ks, ks == 0, ks == 3, qkv_slot(g))
                else:
                    unit(pos // 4, pos % 4, 4 * ks, ks == 0, ks == 3, h_hi, h_lo, qkv_slot(g),
                         h_need=0 if hg == 0 else None)

            mod_sum(1, 0, 0)
            for pos in range(POS0):
                qkv_product(pos)
                if pos % 3 == 0:
                    forget_logits(pos // 3)
                if pos % 3 == 1:
                    mod_sum(2 * (pos // 3) + 2, 1, 0)
                    mod_sum(2 * (pos // 3) + 3, 0, 0)
            pe.wait_ge(consts, C_MASKS)
            for pos in range(POS0, 48):
                attention_steps(pos)
                qkv_product(pos)
                if pos == 9:
                    forget_logits(3)
            for n, (cg, ks) in enumerate(OUT_UNITS):
                pos = 48 + n
                attention_steps(pos)
                if n == 9:
                    sum_squares(1, 0)
                if n == 10:
                    sum_squares(1, 1)
                if n == 14:
                    sum_squares(1, 2)
                if ks == 0:
                    group_slot_free(G_OUT + cg)
                pe.wait_ge(o_lo, 4 * (ks + 1))
                unit(QUAD_OUT + n // 4, n % 4, 4 * ks, ks == 0, ks == 3, g_hi, g_lo, cg % 2)
            sum_squares(1, 3)
            mod_sum(8 + 15, 0, NH)

            def mlp(l):
                q, g, nrm = QUAD_FFN[l], G_FFN[l], 2 * l + 1
                ch = 24 if l == 0 else 44
                gi = 11 * l
                for g0, n in BLOCKS:
                    last_block = n == 3
                    with_mod = l == 0 or g0 == 0
                    with pe.Fori(0, n) as i:
                        for half in range(2):
                            group_slot_free(g + 2 * i + half)
                            for ks in range(4):
                                unit(q + 2 * i + half, ks, 4 * ks, ks == 0, ks == 3, h_hi, h_lo, half,
                                     h_need=KT * nrm)
                        if with_mod:
                            mod_sum(i + ch, 0, NH)
                    q += 2 * n
                    g += 2 * n
                    if with_mod:
                        ch += n
                    if not last_block:
                        with pe.Fori(0, 2) as i:
                            for half in range(2):
                                group_slot_free(g + 2 * i + half)
                                for ks in range(4):
                                    if l == 0 and half == 1 and ks == 0:
                                        mod_sum(2 * i + ch, 1, NH)
                                    pe.wait_ge(glo_ready, 2 * (gi + g0 + ks + 1))
                                    unit(q + 2 * i + half, ks, 4 * ks, ks == 0, ks == 3, g_hi, g_lo, half)
                            if l == 0:
                                mod_sum(2 * i + (ch + 1), 0, NH)
                        q += 4
                        g += 4
                        if l == 0:
                            ch += 4
                    else:
                        for cg in range(4):
                            group_slot_free(g + cg)
                            for ks in range(3):
                                u = 3 * cg + ks
                                if u in (5, 8, 11):
                                    sum_squares(2 * l + 2, (u - 5) // 3)
                                if l == 0 and u == 5:
                                    mod_sum(ch, 0, NH)
                                pe.wait_ge(glo_ready, 2 * (gi + g0 + ks + 1))
                                unit(q + u // 4, u % 4, 4 * ks, ks == 0, ks == 2, g_hi, g_lo, cg % 2)
                sum_squares(2 * l + 2, 3)

            mlp(0)
            def pool_project(gr):
                group_slot_free(G_POOL + gr)
                unit_tok(QUAD_POOL, gr, 4 * gr, True, True, gr % 2, h_need=2 * KT)

            def pool_tokens(gr):
                pe.wait_ge(bank0_free, G_POOL + gr + 1)
                pe.wait_ge(bank1_free, G_POOL + gr + 1)
                if gr >= 2:
                    pe.wait_ge(pool_res, 2 * gr - 2)
                for t in range(4):
                    z0, z1 = (zs[:, gr % 2, a, t * P:(t + 1) * P] for a in range(QT))
                    o = pool_tile(gr, t)
                    mm(o[:, P:256], z1, pmat[:, gr, 256:384], start=t % 2 == 0, stop=False, skip_group_check=True)
                    i = mm(o, z0, pmat[:, gr, 0:256], start=False, stop=True, skip_group_check=True)
                i.then_inc(pool_y, 1)

            pe.wait_ge(consts, C_POOL)
            pe.wait_ge(mod_ready, 44)
            pool_project(0)
            pool_project(1)
            pool_tokens(0)
            pool_project(2)
            pool_tokens(1)
            pool_project(3)
            pool_tokens(2)
            sum_squares(3, 0)
            sum_squares(3, 1)
            pool_tokens(3)
            sum_squares(3, 2)
            sum_squares(3, 3)
            mlp(1)
            pe.wait_ge(bank1_free, G_FFN[1] + 34)
            for b in range(8):
                a, k0 = b % 2, 4 * (b // 2)
                pe.wait_ge(t_ready, 4 * KT + k0 + 4)
                if b >= 4:
                    pe.wait_ge(y_cp[b % 2], b // 2 - 1)
                for t in range(4):
                    i = nc.tensor.transpose(ps[:, b % 4, t * P:(t + 1) * P],
                                            xT[:, k0 + t, a * P:(a + 1) * P], ident[:, :])
                i.then_inc(y_t, 1)

        @block.scalar
        def _(act):
            def A(o, i, f, **kw):
                return nc.scalar.activation(o, i, f, **kw)

            def split(q, j):
                act.wait_ge(raw_landed[j % 4], 16 * (q + j // 4 + 1))
                for h in range(2):
                    if not (isinstance(q, int) and 8 * q + 2 * j + h < 4):
                        act.wait_ge(sub_used, 8 * q + 2 * j + h - 3)
                    A(w_hi[:, (2 * j + h) % 4, :, :],
                      raw[:, j % 4, h * 1024:(h + 1) * 1024].rearrange("p (k n) -> p k n", k=2),
                      ACT.Copy).then_inc(hi_ready, 1)

            def first_products(c_all, a, red):
                act.wait_ge(*mod_landing(c_all, 0))
                if red is not None:
                    act.wait_ge(mod_red, red)
                for kk in range(2):
                    A(macc[:, a, kk, :], mraw[:, 0, kk, :], ACT.Copy,
                      scale=cond[:, kk:kk + 1]).then_inc(mod_first, 1)

            def squares(n, q):
                if 4 * n + q >= 2:
                    act.wait_ge(sum_done, 4 * n + q - 1)
                if n == 0:
                    act.wait_ge(x_copied, 2 * (q + 1))
                halves = ((0, 2), (2, 4)) if n and q == 3 else ((0, 4),)
                for t0, t1 in halves:
                    if n == 3:
                        act.wait_ge(pool_res, 2 * q + t1 // 2)
                    elif n:
                        act.wait_ge((bank0_free, bank1_free)[t1 // 2 - 1], XG[n] + q + 1)
                    A(sq[:, q % 2, t0:t1, :], xT[:, 4 * q + t0:4 * q + t1, :], ACT.Square).then_inc(sq_ready, 1)

            def root(n):
                act.wait_ge(ms_ready, n + 1)
                A(rstd[:, :], rstd[:, :], ACT.Sqrt).then_inc(rt_ready, 1)

            def modulate(n, tiles=range(KT)):
                l, m = n // 2, n % 2
                sh = 96 * l + (SH2 if m else SH1)
                if n:
                    act.wait_ge(mod_ready, 24 * l + (16 if m else 4))
                for t in tiles:
                    if n == 0 and t % 4 == 0:
                        act.wait_ge(mod_ready, t // 2 + 2)
                    act.wait_ge(t_ready, n * KT + t + 1)
                    A(h_hi[:, t, :], tmpn[:, t % 4, :], ACT.Identity,
                      bias=mods[:, sh + t:sh + t + 1]).then_inc(hhi_ready, 1)

            act.wait_ge(c_t, 1)
            A(cond[:, :], ps[:, 7, 0:KT], ACT.Silu).then_inc(cond_s, 1)
            act.wait_ge(cond_s, 1)
            first_products(0, 1, None)
            for b, (n0, n1) in enumerate(((0, 4), (4, 8), (8, 11))):
                act.wait_ge(prm_t, b + 1)
                for k in range(n0, n1):
                    i = A(prm[:, k * P:k * P + ROWS[k]], ps[:, 4 + b, (k - n0) * P:(k - n0) * P + ROWS[k]],
                          ACT.Copy)
                i.then_inc(prm_ready, 1)
            first_products(1, 0, None)
            for b in range(8):
                act.wait_ge(x_t, b + 1)
                A(xT[:, 2 * b:2 * b + 2, :].rearrange("p a n -> p (a n)"), ps[:, b % 4, :],
                  ACT.Copy).then_inc(x_copied, 1)
            for q in range(4):
                squares(0, q)
            root(0)
            act.wait_ge(s_wf, 32)
            A(wf_hi[:, :, :], wf[:, :, :], ACT.Copy).then_inc(wf_hi_s, 1)
            for cq in range(4):
                if cq < 3:
                    first_products(2 * cq + 2, 1, 2 * cq + 1)
                modulate(0, range(4 * cq, 4 * cq + 4))
                for n in range(3 if cq < 3 else 2):
                    if n == 2:
                        first_products(2 * cq + 3, 0, 2 * cq + 2)
                    split((3 * cq + n) // 4, (3 * cq + n) % 4)

            def softplus_tail(n):
                z, L = att_bank(("z", n)), att[:, n % 2, :]
                act.wait_ge(z_done, n + 1)
                if n >= 2:
                    act.wait_ge(sp_ready, n - 1)
                A(L, z, ACT.Abs).then_inc(sb_act, 1)
                act.wait_ge(sb_act, 2 * n + 1)
                A(L, L, ACT.Exp, scale=-1.0).then_inc(sb_act, 1)
                act.wait_ge(sb_act, 2 * n + 2)
                A(L, L, ACT.Ln, bias=1.0).then_inc(l_ready, 1)

            def softmax_exp(n):
                f = n - NSB
                act.wait_ge(bias_ready, f + 1)
                for a, (lo, hi) in enumerate(((0, P), (P, 384))):
                    A(att[:, f % 4, lo:hi], att[:, f % 4, lo:hi], ACT.Exp, bias=fst[:, 2, f, a:a + 1],
                      accum_out=fst[:, 3, f, a:a + 1]).then_inc(p_exp, 1)

            def softmax_scale(n):
                f = n - NSB
                act.wait_ge(rsum_ready, f + 1)
                act.wait_ge(p_exp, 2 * f + 2)
                for a, (lo, hi) in enumerate(((0, P), (P, 384))):
                    i = A(att[:, f % 4, lo:hi], att[:, f % 4, lo:hi], ACT.Copy, scale=fst[:, 4, f, a:a + 1])
                i.then_inc(p_ready, 1)

            def stick_weights(n):
                act.wait_ge(att_free, ALLOC[("z", n)] + 1)
                A(weights_buf(n), weights_buf(n), ACT.Exp).then_inc(w_ready, 1)

            def head_hi(n):
                act.wait_ge(o_done, n + 1)
                A(g_hi[:, n, :], out_bank(n), ACT.Copy).then_inc(o_hi, 1)

            def attention_steps(pos):
                if pos == 11:
                    act.wait_ge(f_dve, 1)
                    A(fg[:, 1], fg[:, 0], ACT.Abs).then_inc(f_act, 1)
                    act.wait_ge(f_act, 1)
                    A(fg[:, 2], fg[:, 1], ACT.Exp, scale=-1.0).then_inc(f_act, 1)
                    act.wait_ge(f_act, 2)
                    A(fg[:, 3], fg[:, 2], ACT.Ln, bias=1.0).then_inc(f_act, 1)
                for kind, n in SCHED.get(pos, []):
                    if kind == "z":
                        (softplus_tail if n < NSB else softmax_exp)(n)
                    elif kind == "c" and n < NSB:
                        stick_weights(n)
                    elif kind == "o":
                        head_hi(n)
                for kind, n in SCHED.get(pos, []):
                    if kind == "z" and n >= NSB:
                        softmax_scale(n)

            for pos in range(POS0, 64):
                attention_steps(pos)
                for ch, j in mod_at(pos):
                    if j == 0:
                        first_products(ch, (ch + 1) % 2, ch - 1)
                if pos < 63:
                    split((pos + 2) // 4, (pos + 2) % 4)
                g = qkv_done(pos)
                if g is not None:
                    hg, kind, _ks = qkv_unit(pos)
                    dst = {"k": kT, "q": qT, "v": vv}[kind].rearrange("p a b -> p (a b)")
                    act.wait_ge(sub_used, 2 * pos + 2)
                    if hg:
                        if kind == "v":
                            act.wait_ge(o_done, 4 * hg)
                        else:
                            act.wait_ge(z_done, 4 * hg)
                    for b, bank_free in enumerate((bank0_free, bank1_free)):
                        A(dst[:, 512 * b:512 * b + 512], ps[:, 2 * qkv_slot(g) + b, :], ACT.Copy,
                          scale=SCALE if kind == "q" else 1.0).then_inc(bank_free, 1)
                n = pos - 48
                if n in (6, 7, 11, 15):
                    squares(1, {6: 0, 7: 1, 11: 2, 15: 3}[n])
            split(16, 1)

            def conv_last_tap(l, used, dst, first_tile, slot, need):
                act.wait_ge(sub_used, used)
                act.wait_ge(gg_ready, need)
                for t in range(4):
                    A(dst[:, t, :], bank_tile(slot, t), ACT.Identity,
                      scale=prm[:, ds(first_tile + CWcol(l, 2) + t, 1)],
                      bias=prm[:, ds(first_tile + CBcol(l) + t, 1)]).then_inc(conv_act, 1)

            def mlp(l):
                q, g, gi = QUAD_FFN[l], G_FFN[l], 11 * l
                ch = 24 if l == 0 else 44
                for g0, n in BLOCKS:
                    with_mod = l == 0 or g0 == 0
                    with act.Fori(0, n) as i:
                        for half in range(2):
                            for ks in range(4):
                                j = 4 * half + ks
                                if with_mod and j == 1:
                                    first_products(i + ch, 0, i + ch)
                                split(q + 2 * i, j + 2)
                                if ks == 3:
                                    conv_last_tap(l, 8 * q + 16 * i + 8 * (half + 1), (ya, yg)[half],
                                                  4 * i + (4 * g0 + FT * half), half,
                                                  2 * i + (2 * (gi + g0) + 1))
                        for b in range(2):
                            act.wait_ge((bank0_free, bank1_free)[b], g + 2 * i + 2)
                            A(yg[:, 2 * b:2 * b + 2, :], yg[:, 2 * b:2 * b + 2, :], ACT.Silu).then_inc(silu_done, 1)
                        for b in range(2):
                            act.wait_ge(gg_ready, 2 * i + (2 * (gi + g0) + b + 2))
                            A(g_hi[:, ds(4 * i + 2 * b, 2), :], yg[:, 2 * b:2 * b + 2, :],
                              ACT.Copy).then_inc(ghi_ready, 1)
                    q += 2 * n
                    g += 2 * n
                    if with_mod:
                        ch += n
                    if n == 4:
                        with act.Fori(0, 2) as i:
                            for j in range(8):
                                if l == 0 and j % 4 == 0:
                                    a = 1 if j < 4 else 0
                                    first_products(2 * i + (ch + (1 - a)), a, 2 * i + (ch - a))
                                split(q + 2 * i, j + 2)
                        q += 4
                        g += 4
                        if l == 0:
                            ch += 4
                    else:
                        for u in range(12):
                            if l == 0 and u == 0:
                                first_products(ch, 0, ch)
                            if u < 11 and 4 * q + u + 2 < UNITS:
                                split(q + (u + 2) // 4, (u + 2) % 4)
                            if u % 3 == 2:
                                squares(2 * l + 2, u // 3)
                        if l == 0:
                            split(q + 3, 1)

            root(1)
            modulate(1)
            mlp(0)
            root(2)
            modulate(2)
            for u in range(4):
                split(QUAD_POOL + (u + 2) // 4, (u + 2) % 4)
                act.wait_ge(sub_used, 8 * QUAD_POOL + 2 * u + 2)
                if u >= 2:
                    act.wait_ge(pool_y, u - 1)
                A(zs[:, u % 2, 0, :], ps[:, 2 * (u % 2), :], ACT.Copy).then_inc(bank0_free, 1)
            for q in range(4):
                squares(3, q)
            root(3)
            modulate(3)
            mlp(1)
            root(4)
            for b in range(0, 8, 2):
                act.wait_ge(y_t, b + 1)
                A(o_tok[:, 0, 256 * b:256 * b + 512], ps[:, b % 4, :], ACT.Copy).then_inc(y_cp[0], 1)

        @block.vector
        def _(dve):
            V = nc.vector
            steps = [0]

            def step(ins):
                ins.then_inc(dve_step, 1)
                steps[0] += 1
                dve.wait_ge(dve_step, steps[0])

            def split(q, j, halves=(0, 1)):
                for h in halves:
                    dve.wait_ge(hi_ready, 8 * q + 2 * j + h + 1)
                    if not (isinstance(q, int) and 8 * q + 2 * j + h < 4):
                        dve.wait_ge(sub_used, 8 * q + 2 * j + h - 3)
                    s = (2 * j + h) % 4
                    V.tensor_tensor(w_lo[:, s, :, :],
                                    raw[:, j % 4, h * 1024:(h + 1) * 1024].rearrange("p (k n) -> p k n", k=2),
                                    w_hi[:, s, :, :].bitcast(F32), ALU.subtract).then_inc(lo_ready, 1)

            def piece(c_all, j, a):
                if j:
                    dve.wait_ge(*mod_landing(c_all, j))
                    for kk in range(2):
                        k = 2 * j + kk
                        if j == 1:
                            dve.wait_ge(mod_first, 2 * c_all + kk + 1)
                        else:
                            dve.wait_ge(mod_acc, 14 * c_all + k - 3)
                        V.scalar_tensor_tensor(macc[:, a, kk, :], mod_slot(c_all, j)[:, kk, :],
                                               cond[:, k:k + 1], macc[:, a, kk, :],
                                               ALU.mult, ALU.add).then_inc(mod_acc, 1)
                if j == 7:
                    dve.wait_ge(mod_acc, 14 * c_all + 14)
                    V.tensor_tensor(macc[:, a, 0, :], macc[:, a, 0, :], macc[:, a, 1, :],
                                    ALU.add).then_inc(mod_added, 1)

            def mod_bias(c_all, l, c_l):
                dve.wait_ge(mod_red, c_all + 1)
                V.tensor_tensor(mods[:, ds(4 * c_l + 96 * l, 4)], ps[:, 7, 256:260],
                                prm[:, ds(P * (1 + l) + 4 * c_l, 4)], ALU.add).then_inc(mod_ready, 1)

            def norm_scale(n):
                dve.wait_ge(sum_done, 4 * n + 4)
                if n:
                    dve.wait_ge(t_ready, n * KT)
                V.tensor_scalar(rstd[:, :], ps[:, SUM_BANK[n], 0:SEQ], 1.0 / D, EPS, ALU.mult, ALU.add).then_inc(ms_ready, 1)

            def norm_gain_vec(n, k0=0, k1=KT):
                l, m = n // 2, n % 2
                dve.wait_ge(mod_ready, k1 // 2 if n == 0 else 24 * l + (20 if m else 8))
                sc = 96 * l + (SC2 if m else SC1)
                step(V.tensor_scalar(amul[:, n, k0:k1], mods[:, sc + k0:sc + k1], 1.0, None, ALU.add))
                step(V.tensor_tensor(amul[:, n, k0:k1], amul[:, n, k0:k1],
                                     prm[:, GAIN + KT * n + k0:GAIN + KT * n + k1], ALU.mult))

            def rstd_finish(n):
                dve.wait_ge(rt_ready, n + 1)
                step(V.reciprocal(rstd[:, :], rstd[:, :]))

            def scaled(n, t):
                if t >= 4:
                    dve.wait_ge(hhi_ready, n * KT + t - 3)
                    dve.wait_ge(hlo_ready, n * KT + t - 3)
                V.scalar_tensor_tensor(tmpn[:, t % 4, :], xT[:, t, :], amul[:, n, t:t + 1], rstd[:, :],
                                       ALU.mult, ALU.mult).then_inc(t_ready, 1)

            def h_rest(n, t):
                sh = 96 * (n // 2) + (SH2 if n % 2 else SH1)
                dve.wait_ge(t_ready, n * KT + t + 1)
                dve.wait_ge(hhi_ready, n * KT + t + 1)
                V.scalar_tensor_tensor(h_lo[:, t, :], tmpn[:, t % 4, :], mods[:, sh + t:sh + t + 1],
                                       h_hi[:, t, :].bitcast(F32), ALU.add,
                                       ALU.subtract).then_inc(hlo_ready, 1)

            def modulate(n, k0=0):
                if n == 3:
                    dve.wait_ge(pool_res, 8)
                elif n:
                    dve.wait_ge(bank1_free, XG[n] + 4)
                for t in range(k0, KT + 2):
                    if t < KT:
                        scaled(n, t)
                    if t >= k0 + 2:
                        h_rest(n, t - 2)

            def residual(g, used, slot, gate, tile0):
                dve.wait_ge(sub_used, used)
                dve.wait_ge(bank1_free, g)
                for t in range(4):
                    i = V.scalar_tensor_tensor(xT[:, ds(tile0 + t, 1), :].rearrange("p a n -> p (a n)"),
                                               bank_tile(slot, t), gate(tile0 + t),
                                               xT[:, ds(tile0 + t, 1), :].rearrange("p a n -> p (a n)"),
                                               ALU.mult, ALU.add)
                    if t % 2:
                        i.then_inc((bank0_free, bank1_free)[t // 2], 1)

            def add_squares(n, q):
                dve.wait_ge(sq_ready, sq_count(n, q))
                v = sq[:, q % 2]
                V.tensor_tensor(v[:, 0:2], v[:, 0:2], v[:, 2:4], ALU.add).then_inc(sq_half, 1)
                dve.wait_ge(sq_half, ADDED[(n, q)])
                V.tensor_tensor(v[:, 0], v[:, 0], v[:, 1], ALU.add).then_inc(sq_added, 1)

            HALF_AT = (5, 6, 7, 8, 12, 13)
            dve.wait_ge(cond_s, 1)
            for ch in range(8):
                for j in range(8):
                    piece(ch, j, (ch + 1) % 2)
                    if ch == 1 and j == 6:
                        dve.wait_ge(prm_ready, 3)
                        mod_bias(0, 0, first_chunk(0))
                        norm_scale(0)
                    if ch >= 2 and ch % 2 == 0 and j == 2 or ch >= 3 and ch % 2 and j == 6:
                        mod_bias(ch - 1, 0, first_chunk(ch - 1))
                    if ch == 2 and j == 0:
                        rstd_finish(0)
                    if ch == 2 and j == 0:
                        dve.wait_ge(wf_hi_s, 1)
                        V.tensor_tensor(wf_lo[:, :, :], wf[:, :, :], wf_hi[:, :, :].bitcast(F32),
                                        ALU.subtract).then_inc(wf_split, 1)
                    if ch < 2:
                        continue
                    cq, at = ch // 2 - 1, 8 * (ch % 2) + j
                    if at == 2:
                        norm_gain_vec(0, 4 * cq, 4 * cq + 4)
                    if 2 <= at < 6:
                        scaled(0, 4 * cq + at - 2)
                    if 3 <= at < 7:
                        h_rest(0, 4 * cq + at - 3)
                    if at in HALF_AT:
                        pos, h = 3 * cq + HALF_AT.index(at) // 2, HALF_AT.index(at) % 2
                        split(pos // 4, pos % 4, (h,))
            mod_bias(7, 0, first_chunk(7))
            norm_gain_vec(0, 12, 16)
            modulate(0, 12)
            split(2, 1)
            split(2, 2)

            def stick_softplus(n):
                spn = att[:, 2 + n % 2, :]
                dve.wait_ge(l_ready, n + 1)
                if n >= 2:
                    dve.wait_ge(cum_done, n - 1)
                step(V.scalar_tensor_tensor(spn, att_bank(("z", n)), 0.0, att[:, n % 2, :], ALU.max, ALU.add))
                V.tensor_tensor(spn, spn, keep[:, :], ALU.mult).then_inc(sp_ready, 1)

            def stick_exponent(n):
                dve.wait_ge(cum_done, n + 1)
                if n >= 2:
                    dve.wait_ge(o_done, n - 1)
                V.scalar_tensor_tensor(weights_buf(n), att_bank(("z", n)), 0.0, drop[:, :],
                                       ALU.min, ALU.add).then_inc(att_free, 1)

            def softmax_bias(n):
                f = n - NSB
                pb = att[:, f % 4, :]
                dve.wait_ge(z_done, n + 1)
                if f >= 4:
                    dve.wait_ge(cum_done, n - 3)
                elif f >= 2:
                    dve.wait_ge(cum_done, NSB)
                V.tensor_tensor(pb, att_bank(("z", n)), dropf[:, :], ALU.add).then_inc(att_free, 1)
                dve.wait_ge(att_free, ALLOC[("z", n)] + 1)
                V.reduce_max(fst[:, 0, f, 0:1], pb[:, 0:P], AX_X)
                step(V.reduce_max(fst[:, 0, f, 1:2], pb[:, P:384], AX_X))
                step(V.tensor_tensor(fst[:, 1, f, :], fst[:, 0, f, :], Fq[:, f, :], ALU.add))
                V.tensor_tensor(fst[:, 2, f, :], Fq[:, f, :], fst[:, 1, f, :],
                                ALU.subtract).then_inc(bias_ready, 1)

            def softmax_rsum(n):
                f = n - NSB
                dve.wait_ge(p_exp, 2 * f + 2)
                V.reciprocal(fst[:, 4, f, :], fst[:, 3, f, :]).then_inc(rsum_ready, 1)

            def take_flipped(n):
                dve.wait_ge(cum_done, n + 1)
                dve.wait_ge(o_done, max(n - 3, NSB))
                V.tensor_copy(weights_buf(n), att_bank(("c", n))).then_inc(att_free, 1)

            def head_lo(n):
                dve.wait_ge(o_hi, n + 1)
                V.tensor_tensor(g_lo[:, n, :], out_bank(n), g_hi[:, n, :].bitcast(F32),
                                ALU.subtract).then_inc(o_lo, 1)

            def attention_steps(pos):
                if pos == 10:
                    dve.wait_ge(f_done, 1)
                    dve.wait_ge(s_wf, 32)
                    for a in range(QT):
                        i = V.scalar_tensor_tensor(fg[:, 0, a, :], ps[:, 6, a * NF:(a + 1) * NF], -1.0,
                                                   bfb[:, :], ALU.mult, ALU.subtract)
                    i.then_inc(f_dve, 1)
                if pos == 12:
                    dve.wait_ge(f_act, 3)
                    V.scalar_tensor_tensor(nls[:, :, :], fg[:, 0], 0.0, fg[:, 3],
                                           ALU.max, ALU.add).then_inc(f_dve, 1)
                if pos == 13:
                    dve.wait_ge(f_done, 2)
                    for a in range(QT):
                        i = V.tensor_scalar(Fq[:, :, a], ps[:, 6, a * NF:(a + 1) * NF], -1.0, None, ALU.mult)
                    i.then_inc(f_dve, 1)
                todo = SCHED.get(pos, [])
                for kind, n in todo:
                    if kind == "c" and n < NSB:
                        stick_exponent(n)
                for kind, n in todo:
                    if kind == "z" and n < NSB:
                        stick_softplus(n)
                    elif kind == "z":
                        softmax_bias(n)
                for kind, n in todo:
                    if kind == "c" and n >= NSB:
                        take_flipped(n)
                for kind, n in todo:
                    if kind == "z" and n >= NSB:
                        softmax_rsum(n)
                    elif kind == "o":
                        head_lo(n)

            def gate_at(l, col):
                return lambda t: mods[:, ds(96 * l + col + t, 1)]

            dve.wait_ge(consts, C_MASKS)
            for pos in range(POS0, 64):
                if pos == 14:
                    dve.wait_ge(f_dve, 3)
                attention_steps(pos)
                if mod_sum_at(pos) is not None:
                    mod_bias(mod_sum_at(pos), 0, mod_sum_at(pos))
                for ch, j in mod_at(pos):
                    piece(ch, j, (ch + 1) % 2)
                if pos - 48 in (7, 8, 12):
                    add_squares(1, {7: 0, 8: 1, 12: 2}[pos - 48])
                if pos < 63:
                    split((pos + 2) // 4, (pos + 2) % 4)
                n = pos - 48
                if n in (6, 7, 11, 15):
                    cg = {6: 0, 7: 1, 11: 2, 15: 3}[n]
                    if cg == 0:
                        dve.wait_ge(mod_ready, 12)
                    residual(G_OUT + cg, 2 * (pos + 1), cg % 2, gate_at(0, G1), 4 * cg)
            split(16, 1)

            def conv_taps(l, dst, first_tile, slot, c0):
                for b in range(2):
                    dve.wait_ge(conv_act, c0 + 2 * b + 2)
                    for tap, sh in ((1, 1), (0, 2)):
                        for t in (2 * b, 2 * b + 1):
                            if tap == 0:
                                dve.wait_ge(conv_tap, c0 + t + 1)
                            i = V.scalar_tensor_tensor(
                                dst[:, t, sh:SEQ], bank_tile(slot, t)[:, 0:SEQ - sh],
                                prm[:, ds(first_tile + CWcol(l, tap) + t, 1)], dst[:, t, sh:SEQ],
                                ALU.mult, ALU.add)
                            if tap == 1:
                                i.then_inc(conv_tap, 1)
                    i.then_inc((bank0_free, bank1_free)[b], 1)

            def mlp(l):
                q, g, gi = QUAD_FFN[l], G_FFN[l], 11 * l
                ch = 24 if l == 0 else 44
                gate = gate_at(l, G2)
                for g0, n in BLOCKS:
                    with_mod = l == 0 or g0 == 0
                    last_block = n == 3
                    with dve.Fori(0, n) as i:
                        for half in range(2):
                            for ks in range(4):
                                j = 4 * half + ks
                                if with_mod and j in (1, 2, 5, 6):
                                    p0 = 2 * (1, 2, 5, 6).index(j)
                                    for p in (p0, p0 + 1):
                                        piece(i + ch, p, 0)
                                split(q + 2 * i, j + 2)
                                if ks == 3:
                                    conv_taps(l, (ya, yg)[half], 4 * i + (4 * g0 + FT * half), half,
                                              8 * i + (8 * (gi + g0) + 4 * half))
                        for b in range(2):
                            dve.wait_ge(silu_done, 2 * i + (2 * (gi + g0) + b + 1))
                            dve.wait_ge((bank0_free, bank1_free)[b], g + 2 * i + 1)
                            V.tensor_tensor(yg[:, 2 * b:2 * b + 2, :], yg[:, 2 * b:2 * b + 2, :],
                                            ya[:, 2 * b:2 * b + 2, :], ALU.mult).then_inc(gg_ready, 1)
                        for b in range(2):
                            dve.wait_ge(ghi_ready, 2 * i + (2 * (gi + g0) + b + 1))
                            V.tensor_tensor(g_lo[:, ds(4 * i + 2 * b, 2), :], yg[:, 2 * b:2 * b + 2, :],
                                            g_hi[:, ds(4 * i + 2 * b, 2), :].bitcast(F32),
                                            ALU.subtract).then_inc(glo_ready, 1)
                        if with_mod:
                            mod_bias(i + ch, 1, i + (ch - 24))
                    q += 2 * n
                    g += 2 * n
                    if with_mod:
                        ch += n
                    if g0 == 0:
                        dve.wait_ge(mod_ready, 24 * (l + 1))
                    if not last_block:
                        with dve.Fori(0, 2) as i:
                            for j in range(8):
                                if l == 0 and j == 4:
                                    mod_bias(2 * i + ch, 1, 2 * i + (ch - 24))
                                if l == 0 and j % 4 < 3:
                                    a = 1 if j < 4 else 0
                                    for p in ((0, 1, 2), (3, 4, 5), (6, 7))[j % 4]:
                                        piece(2 * i + (ch + (1 - a)), p, a)
                                split(q + 2 * i, j + 2)
                                if j % 4 == 3:
                                    residual(g + 2 * i + j // 4, 8 * q + 16 * i + 2 * j + 2, j // 4, gate,
                                             8 * i + 4 * (j // 4))
                                if l == 0 and j == 7:
                                    mod_bias(2 * i + (ch + 1), 1, 2 * i + (ch - 23))
                        q += 4
                        g += 4
                        if l == 0:
                            ch += 4
                    else:
                        for u in range(12):
                            if l == 0 and u == 5:
                                mod_bias(ch, 1, ch - 24)
                            if l == 0 and u < 4:
                                for p in (2 * u, 2 * u + 1):
                                    piece(ch, p, 0)
                            if u in (3, 6, 9):
                                add_squares(2 * l + 2, u // 3 - 1)
                            if u < 11 and 4 * q + u + 2 < UNITS:
                                split(q + (u + 2) // 4, (u + 2) % 4)
                            if u % 3 == 2:
                                cg = u // 3
                                residual(g + cg, 8 * q + 2 * u + 2, cg % 2, gate, 4 * cg)
                        if l == 0:
                            split(q + 3, 1)

            norm_scale(1)
            norm_gain_vec(1)
            rstd_finish(1)
            modulate(1)
            mod_bias(23, 0, 23)
            dve.sem_inc(gg_ready, 1)
            mlp(0)
            norm_scale(2)
            norm_gain_vec(2)
            rstd_finish(2)
            dve.wait_ge(mod_ready, 24 + 12)
            step(V.tensor_tensor(gps[:, :], mods[:, 96 + G1:96 + G1 + KT], prm[:, PSC:PSC + KT], ALU.mult))
            modulate(2)

            def pool_residual(gr):
                dve.wait_ge(pool_y, gr + 1)
                for t in range(4):
                    k = 4 * gr + t
                    i = V.scalar_tensor_tensor(xT[:, k, :], pool_tile(gr, t), gps[:, k:k + 1], xT[:, k, :],
                                               ALU.mult, ALU.add)
                    if t % 2:
                        i.then_inc(pool_res, 1)

            for u in range(4):
                split(QUAD_POOL + (u + 2) // 4, (u + 2) % 4)
                dve.wait_ge(sub_used, 8 * QUAD_POOL + 2 * u + 2)
                if u >= 2:
                    dve.wait_ge(pool_y, u - 1)
                V.tensor_copy(zs[:, u % 2, 1, :], ps[:, 2 * (u % 2) + 1, :]).then_inc(bank1_free, 1)
                if u:
                    pool_residual(u - 1)
            pool_residual(3)
            norm_scale(3)
            norm_gain_vec(3)
            rstd_finish(3)
            modulate(3)
            mlp(1)
            norm_scale(4)
            rstd_finish(4)
            dve.wait_ge(bank1_free, XG[4] + 4)
            for t in range(KT):
                V.scalar_tensor_tensor(xT[:, t, :], xT[:, t, :], prm[:, FGAIN + t:FGAIN + t + 1], rstd[:, :],
                                       ALU.mult, ALU.mult).then_inc(t_ready, 1)
            for b in range(1, 8, 2):
                dve.wait_ge(y_t, b + 1)
                V.tensor_copy(o_tok[:, 1, 256 * (b - 1):256 * (b - 1) + 512], ps[:, b % 4, :]).then_inc(y_cp[1], 1)


_INS = ["x", "c", "w_mod", "b_mod", "norm_gain", "w_attn_in", "b_forget", "w_attn_out", "w_pool",
        "pool_scale", "w_up", "conv_w", "conv_b", "w_down", "final_gain"]


def kernel(**inputs):
    import numpy as np
    import concourse.bacc as bacc
    from concourse import mybir as mb
    from concourse.bass_utils import run_bass_kernel_spmd

    nc = bacc.Bacc("TRN2", target_bir_lowering=False, num_devices=1, dynamic_dma_scratch_size=8192)
    arrays, args = {}, []
    for name in _INS:
        a = np.ascontiguousarray(inputs[name])
        arrays[f"in_{name}"] = a
        args.append(nc.dram_tensor(f"in_{name}", a.shape, mb.dt.from_np(a.dtype), kind="ExternalInput").ap())
    shape = tuple(inputs["x"].shape)
    args.append(nc.dram_tensor("out_0", shape, mb.dt.from_np(np.dtype("float32")), kind="ExternalOutput").ap())
    decoder_trunk(nc, *args)
    r = run_bass_kernel_spmd(nc, [arrays], core_ids=[0])
    return r.results[0]["out_0"]
```
